# Optimizing a Trainium2 kernel written in Bass

```python
import jax, jax.numpy as jnp
from jax import lax
import numpy as np

D_MODEL = 2048
BATCH = 1
SEQ = 512
DEPTH = 1

D_PLE = 256
RMS_EPS = 1e-6
POOL_WINDOWS = (2, 4, 8, 16)
N_POOL_GROUPS = 4
POOL_GROUP_DIM = 128
D_POOL = N_POOL_GROUPS * POOL_GROUP_DIM
N_HEADS = 12
QK_NOPE_DIM = 128
QK_ROPE_DIM = 64
QK_HEAD_DIM = QK_NOPE_DIM + QK_ROPE_DIM
V_HEAD_DIM = 128
Q_LORA_RANK = 512
KV_LORA_RANK = 512
D_ATTN = N_HEADS * V_HEAD_DIM
ROPE_THETA = 10000.0
Q_BLOCK = 128
D_MIX = D_POOL + D_ATTN
D_IN = D_POOL + Q_LORA_RANK + KV_LORA_RANK + QK_ROPE_DIM
PEER_HEADS = 8
PEER_N_KEYS = 128
PEER_N_EXPERTS = PEER_N_KEYS * PEER_N_KEYS
PEER_TOPK = 16
PEER_HALF_DIM = 128
PEER_QUERY_DIM = 2 * PEER_HALF_DIM
PEER_TOKEN_CHUNK = 128
PEER_V_SCALE = 0.5

kernel_name = "hymba_pool_mla_peer_block"

def rmsnorm(x, g):
    xf = x.astype(jnp.float32)
    y = xf * lax.rsqrt(jnp.mean(xf * xf, axis=-1, keepdims=True) + RMS_EPS)
    return (y * g.astype(jnp.float32)).astype(x.dtype)

def rope_tables(positions):
    inv_freq = ROPE_THETA ** (-jnp.arange(0, QK_ROPE_DIM, 2, dtype=jnp.float32) / QK_ROPE_DIM)
    ang = positions.astype(jnp.float32)[..., None] * inv_freq
    return jnp.cos(ang), jnp.sin(ang)

def apply_rope(x, cos, sin):
    half = x.shape[-1] // 2
    x1, x2 = x[..., :half], x[..., half:]
    c = cos.astype(x.dtype)
    s = sin.astype(x.dtype)
    return jnp.concatenate([x1 * c - x2 * s, x2 * c + x1 * s], axis=-1)

def pool_mixer(xp, pool_w, pool_scale):
    b, s, _ = xp.shape
    xg = xp.astype(jnp.float32).reshape(b, s, N_POOL_GROUPS, POOL_GROUP_DIM)
    csum = jnp.cumsum(xg, axis=1)
    t = jnp.arange(s)
    outs = []
    for gi, w in enumerate(POOL_WINDOWS):
        c = csum[:, :, gi]
        lag = jnp.pad(c[:, :s - w], ((0, 0), (w, 0), (0, 0)))
        cnt = jnp.minimum(t + 1, w).astype(jnp.float32)[None, :, None]
        outs.append((c - lag) / cnt - xg[:, :, gi])
    pooled = jnp.stack(outs, axis=2).astype(xp.dtype)
    mixed = jnp.einsum('bsgc,gcd->bsgd', pooled, pool_w).reshape(b, s, D_POOL)
    return mixed * pool_scale

def mla_attention(q_c, kv_c, k_r, q_norm_g, w_uq, kv_norm_g, w_ukv, cos, sin):
    b, s, _ = q_c.shape
    q = (rmsnorm(q_c, q_norm_g) @ w_uq).reshape(b, s, N_HEADS, QK_HEAD_DIM)
    q_nope = q[..., :QK_NOPE_DIM]
    q_rope = apply_rope(q[..., QK_NOPE_DIM:], cos[:, :, None], sin[:, :, None])
    kv = (rmsnorm(kv_c, kv_norm_g) @ w_ukv).reshape(b, s, N_HEADS, QK_NOPE_DIM + V_HEAD_DIM)
    k_nope = kv[..., :QK_NOPE_DIM]
    v = kv[..., QK_NOPE_DIM:]
    k_rope = apply_rope(k_r, cos, sin)
    scale = QK_HEAD_DIM ** -0.5
    outs = []
    for qb in range(s // Q_BLOCK):
        q0 = qb * Q_BLOCK
        kend = q0 + Q_BLOCK
        sc = (jnp.einsum('bqhd,bkhd->bhqk', q_nope[:, q0:kend], k_nope[:, :kend])
              + jnp.einsum('bqhr,bkr->bhqk', q_rope[:, q0:kend], k_rope[:, :kend]))
        sc = sc.astype(jnp.float32) * scale
        causal = jnp.arange(kend)[None, :] <= (q0 + jnp.arange(Q_BLOCK))[:, None]
        sc = jnp.where(causal, sc, jnp.float32(-1e30))
        pr = jax.nn.softmax(sc, axis=-1).astype(v.dtype)
        outs.append(jnp.einsum('bhqk,bkhd->bqhd', pr, v[:, :kend]))
    o = jnp.concatenate(outs, axis=1)
    return o.reshape(b, s, D_ATTN)

def peer_ffn(xn, wq, sub_keys, u, v):
    b, s, d = xn.shape
    t = b * s
    xt = xn.reshape(t, d)
    q = (xt @ wq).reshape(t, PEER_HEADS, 2, PEER_HALF_DIM)
    sc = jnp.einsum('thpc,hpnc->thpn', q, sub_keys).astype(jnp.float32)
    top_v, top_i = lax.top_k(sc, PEER_TOPK)
    kk = PEER_TOPK * PEER_TOPK
    cand_v = (top_v[:, :, 0, :, None] + top_v[:, :, 1, None, :]).reshape(t, PEER_HEADS, kk)
    cand_id = (top_i[:, :, 0, :, None] * PEER_N_KEYS + top_i[:, :, 1, None, :]).reshape(t, PEER_HEADS, kk)
    best_v, best_pos = lax.top_k(cand_v, PEER_TOPK)
    expert = jnp.take_along_axis(cand_id, best_pos, axis=-1)
    gate = jax.nn.softmax(best_v, axis=-1).astype(xn.dtype)
    n_chunks = t // PEER_TOKEN_CHUNK

    def chunk_fn(args):
        xc, ec, gc = args
        hc = jnp.einsum('cd,chkd->chk', xc, u[ec])
        ac = gc * jax.nn.gelu(hc)
        return jnp.einsum('chk,chkd->cd', ac, v[ec])

    out = lax.map(chunk_fn, (
        xt.reshape(n_chunks, PEER_TOKEN_CHUNK, d),
        expert.reshape(n_chunks, PEER_TOKEN_CHUNK, PEER_HEADS, PEER_TOPK),
        gate.reshape(n_chunks, PEER_TOKEN_CHUNK, PEER_HEADS, PEER_TOPK)))
    return out.reshape(b, s, d)

def setup_inputs(seed: int = 0) -> dict:
    key = jax.random.key(seed)
    ks = jax.random.split(key, 24)
    f32 = jnp.float32
    nrm = lambda k, shape, sc: jax.random.normal(k, shape, f32) * sc
    gain = lambda k, shape: 1.0 + 0.02 * jax.random.normal(k, shape, f32)
    L = DEPTH
    return {
        "x": jax.random.normal(ks[0], (BATCH, SEQ, D_MODEL), f32),
        "p": jax.random.normal(ks[1], (DEPTH, BATCH, SEQ, D_PLE), f32),
        "positions": jnp.broadcast_to(jnp.arange(SEQ, dtype=jnp.int32), (BATCH, SEQ)),
        "mix_norm_g": gain(ks[2], (L, D_MODEL)),
        "w_in": nrm(ks[3], (L, D_MODEL, D_IN), D_MODEL ** -0.5),
        "pool_w": nrm(ks[4], (L, N_POOL_GROUPS, POOL_GROUP_DIM, POOL_GROUP_DIM), POOL_GROUP_DIM ** -0.5),
        "pool_scale": gain(ks[5], (L, D_POOL)),
        "q_norm_g": gain(ks[6], (L, Q_LORA_RANK)),
        "w_uq": nrm(ks[7], (L, Q_LORA_RANK, N_HEADS * QK_HEAD_DIM), Q_LORA_RANK ** -0.5),
        "kv_norm_g": gain(ks[8], (L, KV_LORA_RANK)),
        "w_ukv": nrm(ks[9], (L, KV_LORA_RANK, N_HEADS * (QK_NOPE_DIM + V_HEAD_DIM)), KV_LORA_RANK ** -0.5),
        "w_o": nrm(ks[10], (L, D_MIX, D_MODEL), D_MIX ** -0.5),
        "ffn_norm_g": gain(ks[11], (L, D_MODEL)),
        "peer_wq": nrm(ks[12], (L, D_MODEL, PEER_HEADS * PEER_QUERY_DIM), D_MODEL ** -0.5),
        "peer_sub_keys": nrm(ks[13], (L, PEER_HEADS, 2, PEER_N_KEYS, PEER_HALF_DIM), PEER_HALF_DIM ** -0.5),
        "peer_u": nrm(ks[14], (L, PEER_N_EXPERTS, D_MODEL), D_MODEL ** -0.5),
        "peer_v": nrm(ks[15], (L, PEER_N_EXPERTS, D_MODEL), PEER_V_SCALE),
        "ple_norm_g": gain(ks[16], (L, D_MODEL)),
        "ple_w_gate": nrm(ks[17], (L, D_MODEL, D_MODEL), D_MODEL ** -0.5),
        "ple_w_proj": nrm(ks[18], (L, D_PLE, D_MODEL), D_PLE ** -0.5),
        "final_norm_g": gain(ks[19], (D_MODEL,)),
    }

def reference(x, p, positions, mix_norm_g, w_in, pool_w, pool_scale, q_norm_g, w_uq,
              kv_norm_g, w_ukv, w_o, ffn_norm_g, peer_wq, peer_sub_keys, peer_u, peer_v,
              ple_norm_g, ple_w_gate, ple_w_proj, final_norm_g):
    cos, sin = rope_tables(positions)
    h = x
    o1 = D_POOL
    o2 = o1 + Q_LORA_RANK
    o3 = o2 + KV_LORA_RANK
    for i in range(DEPTH):
        z = rmsnorm(h, mix_norm_g[i]) @ w_in[i]
        y_pool = pool_mixer(z[..., :o1], pool_w[i], pool_scale[i])
        y_attn = mla_attention(z[..., o1:o2], z[..., o2:o3], z[..., o3:],
                               q_norm_g[i], w_uq[i], kv_norm_g[i], w_ukv[i], cos, sin)
        h = h + jnp.concatenate([y_pool, y_attn], axis=-1) @ w_o[i]
        h = h + peer_ffn(rmsnorm(h, ffn_norm_g[i]), peer_wq[i], peer_sub_keys[i], peer_u[i], peer_v[i])
        gate = jax.nn.sigmoid(rmsnorm(h, ple_norm_g[i]) @ ple_w_gate[i])
        h = h + gate * (p[i] @ ple_w_proj[i])
    return rmsnorm(h, final_norm_g)


_drawn_inputs = setup_inputs


def setup_inputs(seed=0):
    import zlib

    import numpy as np

    out = dict(_drawn_inputs(seed))
    spreads = {}
    factors = {'pool_scale': 18.488,
     'q_norm_g': 5.738,
     'kv_norm_g': 4.477,
     'ple_norm_g': 64.0,
     'final_norm_g': 8.472,
     'ffn_norm_g': 5.907}
    for name, (base, spread) in spreads.items():
        noise = np.random.default_rng([zlib.crc32(name.encode()), seed]).standard_normal(out[name].shape)
        drawn = base * np.exp(spread * noise) if base else spread * noise
        out[name] = __import__('jax').numpy.asarray(drawn.astype(out[name].dtype))
    for name, factor in factors.items():
        out[name] = (out[name] * factor).astype(out[name].dtype)
    return out
```

```python
from contextlib import ExitStack

import concourse.bass as bass
import numpy as np
from concourse import mybir

F32 = mybir.dt.float32
F32R = mybir.dt.float32r
BF16 = mybir.dt.bfloat16
U32 = mybir.dt.uint32
I32 = mybir.dt.int32
ALU = mybir.AluOpType
ACT = mybir.ActivationFunctionType
AX = mybir.AxisListType

P = 128
T = 512
D = 2048
DC = D // P
TC = T // P
EPS = 1e-6
HEADS = 12
LC = 512 // P
QK = 192
SCALE = QK ** -0.5
WINDOWS = (2, 4, 8, 16)
PH = 8
TOPK = 16
NK = 128
HK = PH * TOPK
D_PLE = 256

U_IN = 0
N_IN = 13
U_HEAD = U_IN + N_IN
U_WO = U_HEAD + HEADS
U_WQ = U_WO + DC
U_PEER = U_WQ + 2 * PH
GROUP = 4
N_GROUPS = NK // GROUP
N_PEER = 2 * NK
U_PROJ = U_PEER + N_PEER
U_GATE = U_PROJ + 2
N_UNITS = U_GATE + DC

C_IDENT, C_IOTA, C_MASK, C_DUP = 0, 128, 256, 384
C_GAIN = 512
G_MIX, G_FFN, G_PLE, G_FIN, G_Q, G_KV, G_POOL = (C_GAIN + o for o in (0, 16, 32, 48, 64, 68, 72))
N_GAIN = 76

TB = 32
N_TB = T // TB
OH = 8


def build_block(nc, x_t, p_t, positions, gains, consts, rope_cols, pool_inv, w_in, pool_w, w_head,
                w_o, w_q, keys, u_t, v, w_proj, w_gate, out_t):
    ctx = ExitStack()
    with ctx:
        base = (nc.sbuf_base + 63) // 64 * 64
        g_dram = nc.dram_tensor("gate_matrix", (N_TB, P, NK, TB), F32, kind="Internal").ap()

        def at(name, offset, shape, dtype=F32):
            return nc.alloc_sbuf_tensor_at(name, shape, dtype, offset=base + offset)

        K = 1024
        raw = [at(f"raw{s}", 4 * K * s, [P, 8, P]) for s in range(2)]
        w_hi = [at(f"w_hi{s}", (8 + 8 * s) * K, [P, 16, P], F32R) for s in range(2)]
        w_lo = [at(f"w_lo{s}", (24 + 8 * s) * K, [P, 16, P], F32R) for s in range(2)]
        h_at, one, two, rest = 40 * K, 72 * K, 136 * K, 200 * K
        h = at("h", h_at, [P, DC, T])
        x1_hi = at("x1_hi", one, [P, DC, T], F32R)
        x1_lo = at("x1_lo", one + 32 * K, [P, DC, T], F32R)
        x2_hi = at("x2_hi", two, [P, DC, T], F32R)
        x2_lo = at("x2_lo", two + 32 * K, [P, DC, T], F32R)
        ident = at("ident", rest, [P, P])
        iota = at("iota", rest + 512, [P, P])
        ones = at("ones", rest + K, [P, P])
        ident_b = at("ident_b", rest + K + 512, [P, P], BF16)
        mask_b = at("mask_b", rest + K + 768, [P, P], BF16)
        gain = at("gain", rest + 2 * K, [P, N_GAIN])
        rope_c = at("rope_c", rest + 2 * K + 320, [P, 2])
        p_inv = at("p_inv", rest + 2 * K + 352, [P, 4, 16])
        neg_max = at("neg_max", rest + 2 * K + 640, [P, TC])
        row_sum = at("row_sum", rest + 2 * K + 672, [P, TC])
        row_inv = at("row_inv", rest + 2 * K + 704, [P, TC])
        rinv = at("rinv", rest + 3 * K, [P, T])
        table = at("table", rest + 5 * K, [P, T])
        acc = table

        z = at("z", h_at, [P, N_IN, T])
        win = [at(f"win{i}", h_at + (26 + 2 * i) * K, [P, T]) for i in range(2)]
        sq_x = at("sq_x", two, [P, DC, T])
        x_acc = at("x_acc", two + 32 * K, [P, T])
        pos_i = at("pos_i", two + 34 * K, [P, T], I32)
        ang = at("ang", two + 36 * K, [P, T])
        turn = at("turn", two + 38 * K, [P, T])
        mask_f = at("mask_f", two + 44 * K, [P, P])
        l_hi = [at(f"l_hi{i}", two + 16 * K * i, [P, LC, T], F32R) for i in range(2)]
        l_lo = [at(f"l_lo{i}", two + 16 * K * i + 8 * K, [P, LC, T], F32R) for i in range(2)]
        sq_l = at("sq_l", two + 32 * K, [P, LC, T])
        rinv_l = at("rinv_l", two + 42 * K, [P, T])
        q_n = at("q_n", two + 32 * K, [P, T])
        q_r = at("q_r", two + 34 * K, [P, T])
        k_n = at("k_n", two + 36 * K, [P, T])
        v_h = [at(f"v_h{i}", two + (38 + 2 * i) * K, [P, TC, P]) for i in range(2)]
        prob_t = at("prob_t", two + 42 * K, [P, TC, T])
        prob = at("prob", two + 50 * K, [P, TC * (TC + 1) // 2, P])
        key_p = at("key_p", two + 55 * K, [P, T])
        key_r = at("key_r", two + 57 * K, [P, T])
        pool_wt = at("pool_wt", two + 59 * K, [P, 4, P])
        dup = at("dup", two + 61 * K, [P, P])

        k_all = at("k_all", one, [P, 2 * PH, NK])
        q_f = [at(f"q_f{i}", one + (8 + 2 * i) * K, [P, T]) for i in range(2)]
        s_f = [at(f"s_f{i}", one + (12 + 2 * i) * K, [P, TC, NK]) for i in range(2)]
        s_cut = at("s_cut", one + 16 * K, [P, TC, NK])
        carrier = at("carrier", one + 54 * K, [P, 1])
        cand = at("cand", one + 18 * K, [P, TC, TOPK, TOPK])
        cand_cut = at("cand_cut", one + 22 * K, [P, TC, TOPK * TOPK])
        pick = [at(f"pick{i}", one + (26 + 4 * i) * K, [P, TC * TOPK, TOPK]) for i in range(2)]
        picked = [at(f"picked{i}", one + (34 + 4 * i) * K, [P, TC * TOPK, TOPK]) for i in range(2)]
        sel = [at(f"sel{i}", one + (42 + 2 * i) * K, [P, TC, PH, TOPK]) for i in range(3)]
        t_v = [at(f"t_v{i}", one + 48 * K + 256 * i, [P, TC, TOPK]) for i in range(2)]
        t_i = [at(f"t_i{i}", one + 49 * K + 256 * i, [P, TC, TOPK], U32) for i in range(2)]
        b_v = at("b_v", one + 50 * K, [P, TC, TOPK])
        b_pos = at("b_pos", one + 50 * K + 256, [P, TC, TOPK], U32)
        pos_hl = [at(f"pos_hl{i}", one + 51 * K + 256 * i, [P, TC * TOPK], U32) for i in range(2)]
        b_exp = at("b_exp", one + 52 * K, [P, TC, TOPK])
        b_sum = at("b_sum", one + 52 * K + 256, [P, TC])
        b_inv = at("b_inv", one + 52 * K + 320, [P, TC])
        t_if = [at(f"t_if{i}", one + 53 * K + 256 * i, [P, TC, TOPK]) for i in range(2)]
        hk_t = [at(f"hk_t{i}", one + 2 * K * i, [P, T]) for i in range(3)]
        one_i = [at(f"one_i{i}", one + (6 + 4 * i) * K, [P, OH, NK]) for i in range(2)]
        one_g = [at(f"one_g{i}", one + (14 + 4 * i) * K, [P, OH, NK]) for i in range(2)]
        one_j = [at(f"one_j{i}", one + (22 + 4 * i) * K, [P, OH, NK]) for i in range(2)]
        g_blk = [at(f"g_blk{i}", one + (30 + 16 * i) * K, [P, NK, TB]) for i in range(2)]
        a_hi = [at(f"a_hi{i}", one + 2 * K * i, [P, T], F32R) for i in range(5)]
        a_lo = [at(f"a_lo{i}", one + (10 + 2 * i) * K, [P, T], F32R) for i in range(5)]
        g_tile = [at(f"g_tile{i}", one + (20 + 8 * i) * K, [P, N_TB, GROUP, TB]) for i in range(2)]
        h_s = at("h_s", one + 36 * K, [P, T])
        h_g = at("h_g", one + 38 * K, [P, T])
        h_a = at("h_a", one + 40 * K, [P, T])
        pt = at("pt", one + 44 * K, [P, 2, T])
        pt_hi = at("pt_hi", one + 48 * K, [P, 2, T], F32R)
        pt_lo = at("pt_lo", one + 52 * K, [P, 2, T], F32R)
        proj = at("proj", one, [P, DC, T])
        g_pre = at("g_pre", one + 56 * K, [P, T])
        g_sig = at("g_sig", one + 58 * K, [P, T])
        g_mul = at("g_mul", one + 60 * K, [P, T])

        bank = [ctx.enter_context(nc.psum_tensor(f"bank{i}", [P, T], F32)) for i in range(8)]

        def sem(name):
            return ctx.enter_context(nc.semaphore(name))

        raw_loaded = [sem(f"raw_loaded{s}") for s in range(2)]
        hi_ready = sem("hi_ready")
        lo_ready = sem("lo_ready")
        weights_used = sem("weights_used")
        const_in = sem("const_in")
        small_in = sem("small_in")
        x_in = [sem(f"x_in{i}") for i in range(4)]
        consts_done = sem("consts_done")
        x1_hi_ready = sem("x1_hi_ready")
        x1_ready = sem("x1_ready")
        sq_ready = sem("sq_ready")
        pool_step = sem("pool_step")
        win_step = sem("win_step")
        rope_step = sem("rope_step")
        rope_sin = sem("rope_sin")
        stat_sum, stat_var, stat_std, stat_inv = (sem(f"stat_{n}") for n in ("sum", "var", "std", "inv"))
        in_out = sem("in_out")
        lat_sq = sem("lat_sq")
        lat_norm = sem("lat_norm")
        lat_hi = sem("lat_hi")
        lat_ready = sem("lat_ready")
        key_turned = sem("key_turned")
        key_sum = sem("key_sum")
        key_ready = sem("key_ready")
        pooled = sem("pooled")
        pool_mixed = sem("pool_mixed")
        pool_hi = sem("pool_hi")
        pool_ready = sem("pool_ready")
        x_again = sem("x_again")
        q_done, r_done, k_done = sem("q_done"), sem("r_done"), sem("k_done")
        act_proj = sem("act_proj")
        dve_proj = sem("dve_proj")
        scores_done = sem("scores_done")
        neg_ready = sem("neg_ready")
        exp_ready = sem("exp_ready")
        sum_inv = sem("sum_inv")
        prob_ready = sem("prob_ready")
        turned = sem("turned")
        act_turned, dve_turned = sem("act_turned"), sem("dve_turned")
        mixed = sem("mixed")
        y_hi = sem("y_hi")
        y_ready = sem("y_ready")
        h_ready = sem("h_ready")
        x2_hi_ready = sem("x2_hi_ready")
        x2_ready = sem("x2_ready")
        h_sq = sem("h_sq")
        acc_step = sem("acc_step")
        keys_in = sem("keys_in")
        q_ready = sem("q_ready")
        s_done = sem("s_done")
        s_ready = sem("s_ready")
        topk_step = sem("topk_step")
        pick_ready = sem("pick_ready")
        picked_ready = sem("picked_ready")
        gate_in = sem("gate_in")
        gate_exp = sem("gate_exp")
        hk_turned = sem("hk_turned")
        hk_ready = sem("hk_ready")
        oh_i = sem("oh_i")
        oh_g = sem("oh_g")
        oh_j = sem("oh_j")
        g_done = sem("g_done")
        g_out = sem("g_out")
        g_stored = [sem(f"g_stored{i}") for i in range(2)]
        g_in = [sem(f"g_in{i}") for i in range(2)]
        e_scaled, e_gelu, e_gated, e_hi, e_ready = (
            sem(f"e_{n}") for n in ("scaled", "gelu", "gated", "hi", "ready"))
        v_done = sem("v_done")
        v_added = sem("v_added")
        p_in = sem("p_in")
        p_hi, p_ready = sem("p_hi"), sem("p_ready")
        x3_hi_ready, x3_ready, h3_sq = (sem(f"x3_{n}") for n in ("hi", "ready", "sq"))
        proj_done, act_proj_out, dve_proj_out = sem("proj_done"), sem("act_proj_out"), sem("dve_proj_out")
        gate_pre, gate_sig, gate_mul, h_end = (sem(f"gate_{n}") for n in ("pre", "sig", "mul", "end"))
        end_sq = sem("end_sq")
        fin_ready = sem("fin_ready")
        out_stored = sem("out_stored")

        PER_TOPK = 20
        ROPE_STEPS = 11
        ACC = DC + 1

        def a_slot(m, par):
            return m if m or not par else GROUP

        def chunk(tensor, n):
            if isinstance(n, int):
                return tensor[:, n, :]
            return tensor[:, bass.ds(n, 1), :].rearrange("p a t -> p (a t)")

        def peer_unit(g, k):
            return U_PEER + 1 + 8 * g + k

        def peer_slot(k):
            return (U_PEER + 1 + k) % 2

        block = ctx.enter_context(nc.Block())

        @block.sync
        def _(sp):
            def load_unit(u, halves):
                for s in range(2):
                    if not isinstance(u, int) or u > 0:
                        sp.wait_ge(lo_ready, 2 * u - 1 + s)
                    dst, src = halves(s)
                    sp.dma_start(dst, src).then_inc(raw_loaded[s], 16)

            def packed(w, n):
                return lambda s: (raw[s][:, :, :], w[n, :, 8 * s:8 * s + 8, :])

            def v_part(g, quarter):
                vr = v.rearrange("(g m e) (q c) -> g q e m c", g=N_GROUPS, m=GROUP, q=4)
                return lambda s: (raw[s][:, :, :].rearrange("p (m c) e -> p m (c e)", m=2),
                                  vr[g, quarter, :, 2 * s:2 * s + 2, :])

            sp.dma_start(gain[:, :], gains).then_inc(small_in, 16)
            load_unit(0, packed(w_in, 0))
            for i in range(4):
                sp.dma_start(h[:, 4 * i:4 * i + 4, :], x_t[:, 4 * i:4 * i + 4, :]).then_inc(x_in[i], 16)
            sp.dma_start(ident[:, :], consts[:, C_IDENT:C_IDENT + P]).then_inc(const_in, 16)
            sp.dma_start(iota[:, :], consts[:, C_IOTA:C_IOTA + P]).then_inc(const_in, 16)
            sp.dma_start(mask_f[:, :], consts[:, C_MASK:C_MASK + P]).then_inc(const_in, 16)
            sp.dma_start(dup[:, :], consts[:, C_DUP:C_DUP + P]).then_inc(const_in, 16)
            sp.dma_start(rope_c[:, :], rope_cols).then_inc(const_in, 16)
            sp.dma_start(p_inv[:, :, :], pool_inv).then_inc(const_in, 16)
            sp.dma_start(pool_wt[:, :, :], pool_w).then_inc(const_in, 16)
            sp.dma_start(pos_i[:, :], positions.to_broadcast([P, T])).then_inc(const_in, 16)
            with sp.Fori(1, N_IN) as n:
                load_unit(n, packed(w_in, n))
            load_unit(U_HEAD, packed(w_head, 0))
            load_unit(U_HEAD + 1, packed(w_head, 1))
            sp.wait_ge(pool_mixed, 4)
            for i in range(4):
                sp.dma_start(h[:, 4 * i:4 * i + 4, :], x_t[:, 4 * i:4 * i + 4, :]).then_inc(x_again, 16)
            with sp.Fori(2, HEADS) as n:
                load_unit(n + U_HEAD, packed(w_head, n))
            with sp.Fori(0, DC) as n:
                load_unit(n + U_WO, packed(w_o, n))
            load_unit(U_WQ, packed(w_q, 0))
            sp.wait_ge(weights_used, U_WQ)
            sp.dma_start(k_all[:, :, :], keys).then_inc(keys_in, 16)
            with sp.Fori(1, 2 * PH) as n:
                load_unit(n + U_WQ, packed(w_q, n))
            load_unit(U_PEER, packed(u_t, 0))
            load_unit(U_PEER + 1, packed(u_t, 1))
            with sp.Fori(0, N_TB // 2) as b2:
                for s in range(2):
                    sp.wait_ge(g_out, (TB // OH) * 2 * (2 * b2 + s + 1))
                    sp.dma_start(g_dram[2 * b2 + s], g_blk[s][:, :, :]).then_inc(g_stored[s], 16)
            for s in range(2):
                sp.wait_ge(g_stored[s], 16 * (N_TB // 2))

            def load_g(g, par):
                sp.dma_start(g_tile[par][:, :, :, :],
                             g_dram[:, :, bass.ds(g * GROUP, GROUP), :].rearrange("b j i t -> j b i t")
                             ).then_inc(g_in[par], 16)

            def peer_group(g, par, first=False, last=False):
                for m in range(1, GROUP):
                    if not (first and m == 1):
                        load_unit(peer_unit(g, m - 1), packed(u_t, g * GROUP + m))
                if not last:
                    if not first:
                        sp.wait_ge(e_gated, GROUP * g)
                    load_g(g + 1, 1 - par)
                    load_unit(peer_unit(g, 3), packed(u_t, (g + 1) * GROUP))
                for q in range(4):
                    load_unit(peer_unit(g, 4 + q - (1 if last else 0)), v_part(g, q))

            load_g(0, 0)
            sp.dma_start(pt[:, :, :], p_t).then_inc(p_in, 16)
            peer_group(0, 0, first=True)
            peer_group(1, 1)
            with sp.Fori(1, N_GROUPS // 2 - 1) as g2:
                peer_group(2 * g2, 0)
                peer_group(2 * g2 + 1, 1)
            peer_group(N_GROUPS - 2, 0)
            peer_group(N_GROUPS - 1, 1, last=True)
            for n in range(2):
                load_unit(U_PROJ + n, packed(w_proj, n))
            with sp.Fori(0, DC) as n:
                load_unit(n + U_GATE, packed(w_gate, n))
            for i in range(4):
                sp.wait_ge(fin_ready, 4 * i + 4)
                sp.dma_start(out_t[:, 4 * i:4 * i + 4, :], proj[:, 4 * i:4 * i + 4, :]).then_inc(out_stored, 16)
            sp.wait_ge(out_stored, 64)

        @block.tensor
        def _(pe):
            def passes(out, blk, slot, m_hi, m_lo, first, last):
                pe.matmul(out, w_hi[slot][:, blk, :], m_hi, start=first, stop=False)
                pe.matmul(out, w_hi[slot][:, blk, :], m_lo, start=False, stop=False)
                return pe.matmul(out, w_lo[slot][:, blk, :], m_hi, start=False, stop=last)

            def half_in(u, s):
                pe.wait_ge(lo_ready, 2 * u + 1 + s)

            def unit(u, slot, out, x_hi, x_lo):
                for b in range(16):
                    if b % 8 == 0:
                        half_in(u, b // 8)
                    mm = passes(out[:, :], b, slot, x_hi[:, b, :], x_lo[:, b, :], b == 0, b == 15)
                mm.then_inc(weights_used, 1)

            def in_unit(u, slot):
                if not isinstance(u, int) or u >= 2:
                    pe.wait_ge(in_out, u - 1)
                unit(u, slot, bank[slot], x1_hi, x1_lo)

            pe.wait_ge(x1_ready, DC)
            in_unit(0, 0)
            pe.wait_ge(pool_step, DC - 1)
            pe.matmul(bank[7][:, :], ones[:, :], x_acc[:, :], start=True, stop=True).then_inc(stat_sum, 1)
            with pe.Fori(0, 2) as i:
                in_unit(2 * i + 1, 1)
                in_unit(2 * i + 2, 0)
            in_unit(5, 1)

            def latent_sum(i):
                pe.wait_ge(lat_sq, i + 1)
                pe.wait_ge(stat_var, i + 1)
                for c in range(LC):
                    mm = pe.matmul(bank[7][:, :], ones[:, :], sq_l[:, c, :], start=(c == 0), stop=(c == LC - 1))
                mm.then_inc(stat_sum, 1)

            latent_sum(0)
            with pe.Fori(0, 2) as i:
                in_unit(2 * i + 6, 0)
                in_unit(2 * i + 7, 1)
            latent_sum(1)
            pe.wait_ge(key_turned, 1)
            pe.matmul(bank[6][:, :], dup[:, :], key_p[:, :], start=True, stop=True).then_inc(key_sum, 1)
            in_unit(10, 0)
            in_unit(11, 1)
            in_unit(12, 0)

            def project_head(hd, slot, first=False):
                u = hd + U_HEAD
                for part, (b_out, lat, done) in enumerate(((0, 0, q_done), (1, 0, r_done), (0, 1, k_done))):
                    if part == 0:
                        half_in(u, 0)
                        pe.wait_ge(in_out, N_IN) if first else pe.wait_ge(act_proj, 2 * hd)
                    elif part == 1:
                        None if first else pe.wait_ge(dve_proj, 2 * hd)
                    else:
                        half_in(u, 1)
                        pe.wait_ge(act_proj, 2 * hd + 1)
                    for c in range(LC):
                        mm = passes(bank[b_out][:, :], 4 * part + c, slot, l_hi[lat][:, c, :], l_lo[lat][:, c, :],
                                    c == 0, c == LC - 1)
                    mm.then_inc(done, 1)
                pe.wait_ge(dve_proj, 2 * hd + 1)
                for t in range(TC):
                    ts = slice(t * P, (t + 1) * P)
                    for c in range(LC):
                        out = bank[1][:, ts]
                        pe.matmul(out, l_hi[1][:, c, ts], w_hi[slot][:, 12 + c, :], start=(c == 0), stop=False)
                        pe.matmul(out, l_hi[1][:, c, ts], w_lo[slot][:, 12 + c, :], start=False, stop=False)
                        mm = pe.matmul(out, l_lo[1][:, c, ts], w_hi[slot][:, 12 + c, :], start=False,
                                       stop=(c == LC - 1))
                mm.then_inc(weights_used, 1)

            def scores(hd, first=False):
                pe.wait_ge(act_proj, 2 * hd + 2)
                pe.wait_ge(dve_proj, 2 * hd + 1)
                for t in range(TC):
                    n = (t + 1) * P
                    ts = slice(t * P, n)
                    out = bank[2 + t]
                    if not first:
                        if t == TC - 1:
                            pe.wait_ge(y_ready, hd)
                        pe.wait_ge(exp_ready, 4 * hd - 3 + t)
                    pe.matmul(out[:, 0:n], q_n[:, ts], k_n[:, 0:n], start=True, stop=False)
                    pe.matmul(out[:, 0:n], q_r[:, ts], key_r[:, 0:n], start=False, stop=False)
                    pe.matmul(out[:, ts], ident_b[:, :], mask_b[:, :], start=False, stop=True)\
                      .then_inc(scores_done, 1)

            def mix_head(hd, par):
                for t in range(TC):
                    pe.wait_ge(prob_ready, 4 * hd + t + 1)
                    if t >= 2:
                        pe.wait_ge(dve_turned if t == 2 else act_turned, 2 * hd + 1)
                    out = bank[6 + t % 2]
                    for c in range(t + 1):
                        mm = pe.transpose(out[:, c * P:(c + 1) * P], prob[:, t * (t + 1) // 2 + c, :], ident[:, :])
                    mm.then_inc(turned, 1)
                pe.wait_ge(dve_turned, 2 * hd + 2)
                pe.wait_ge(act_turned, 2 * hd + 2)
                pe.wait_ge(dve_proj, 2 * hd + 2)
                for c in range(TC):
                    mm = pe.matmul(bank[5][:, c * P:T], v_h[par][:, c, :], prob_t[:, c, c * P:T],
                                   start=(c == 0), stop=(c == TC - 1))
                mm.then_inc(mixed, 1)

            pe.wait_ge(lat_ready, 2 * LC)
            pe.wait_ge(key_ready, 1)
            project_head(0, (U_HEAD + 0) % 2, first=True)
            scores(0, first=True)
            for g in range(4):
                pe.wait_ge(pooled, g + 1)
                if g >= 2:
                    pe.wait_ge(pool_ready, g - 1)
                pe.matmul(bank[6 + g % 2][:, :], pool_wt[:, g, :], z[:, 9 + g, :], start=True, stop=True)\
                  .then_inc(pool_mixed, 1)
            pe.wait_ge(pool_ready, 4)
            with pe.Fori(0, (HEADS - 2) // 2) as i:
                for k in range(2):
                    hd = 2 * i + 1 + k
                    project_head(hd, (U_HEAD + 1 + k) % 2)
                    mix_head(hd - 1, k % 2)
                    scores(hd)
            project_head(HEADS - 1, (U_HEAD + HEADS - 1) % 2)
            mix_head(HEADS - 2, 0)
            scores(HEADS - 1)
            mix_head(HEADS - 1, 1)

            pe.wait_ge(y_ready, HEADS)
            for k in range(2):
                unit(k + U_WO, (U_WO + k) % 2, bank[k], x1_hi, x1_lo)
            with pe.Fori(1, DC // 2) as i:
                for k in range(2):
                    pe.wait_ge(h_ready, 2 * i + k - 1)
                    unit(2 * i + k + U_WO, (U_WO + k) % 2, bank[k], x1_hi, x1_lo)

            def key_scores(n, k):
                pe.wait_ge(q_ready, n + 1)
                for t in range(TC):
                    mm = pe.matmul(bank[2 + k][:, t * P:(t + 1) * P], q_f[k][:, t * P:(t + 1) * P],
                                   chunk(k_all, n), start=True, stop=True)
                mm.then_inc(s_done, 1)

            pe.wait_ge(x2_ready, DC)
            unit(U_WQ, U_WQ % 2, bank[0], x2_hi, x2_lo)
            pe.wait_ge(acc_step, ACC)
            pe.matmul(bank[7][:, :], ones[:, :], acc[:, :], start=True, stop=True).then_inc(stat_sum, 1)
            unit(U_WQ + 1, (U_WQ + 1) % 2, bank[1], x2_hi, x2_lo)
            pe.wait_ge(keys_in, 16)
            key_scores(0, 0)

            def query_head(hd):
                for k in range(2):
                    n = 2 * hd + k
                    pe.wait_ge(q_ready, n - 1)
                    unit(n + U_WQ, (U_WQ + k) % 2, bank[k], x2_hi, x2_lo)
                    if not isinstance(n, int) or n > 2:
                        pe.wait_ge(s_ready, n - 2)
                    key_scores(n - 1, (k + 1) % 2)

            query_head(1)
            with pe.Fori(2, PH) as hd:
                query_head(hd)
            pe.wait_ge(s_ready, 2 * PH - 2)
            key_scores(2 * PH - 1, 1)

            pe.wait_ge(topk_step, PER_TOPK * PH)
            pe.wait_ge(s_ready, 2 * PH)
            for i in range(3):
                for t in range(TC):
                    mm = pe.transpose(bank[2 + i][:, t * P:(t + 1) * P],
                                      sel[i][:, t, :, :].rearrange("p h k -> p (h k)"), ident[:, :])
                mm.then_inc(hk_turned, 1)

            def g_group(q, s, first=False):
                pe.wait_ge(oh_g, q + 1)
                pe.wait_ge(oh_j, q + 1)
                for half in range(2):
                    out = bank[6 + half]
                    if not first:
                        pe.wait_ge(g_out, 2 * q - 1 + half)
                    for t in range(4):
                        o = 4 * half + t
                        mm = pe.matmul(out[:, t * P:(t + 1) * P], one_j[s][:, o, :], one_g[s][:, o, :],
                                       start=True, stop=True)
                    mm.then_inc(g_done, 1)

            g_group(0, 0, first=True)
            g_group(1, 1)
            with pe.Fori(1, T // OH // 2) as q2:
                for s in range(2):
                    g_group(2 * q2 + s, s)

            def first_product(j, u, slot, b, first=False):
                if not first:
                    pe.wait_ge(e_scaled, j - 1)
                unit(u, slot, bank[b], x2_hi, x2_lo)

            def second_product(g, par, q, u, slot, first=False):
                if q == 0:
                    pe.wait_ge(e_ready, GROUP * g + GROUP)
                half_in(u, 0)
                half_in(u, 1)
                for c in range(4):
                    if not (first and q == 0):
                        pe.wait_ge(v_added, 16 * g + 4 * q - 3 + c)
                    for m in range(GROUP):
                        a = a_slot(m, par)
                        mm = passes(bank[2 + c][:, :], 4 * m + c, slot, a_hi[a][:, :], a_lo[a][:, :],
                                    m == 0, m == GROUP - 1)
                    mm.then_inc(v_done if c < 3 else weights_used, 1)

            def peer_group(g, par, first=False, last=False):
                for m in range(1, GROUP):
                    first_product(g * GROUP + m, peer_unit(g, m - 1), peer_slot(m - 1), m % 2, first and m == 1)
                if not last:
                    first_product((g + 1) * GROUP, peer_unit(g, 3), peer_slot(3), 0)
                for q in range(4):
                    k = 4 + q - (1 if last else 0)
                    second_product(g, par, q, peer_unit(g, k), peer_slot(k), first)

            first_product(0, U_PEER, U_PEER % 2, 0, first=True)
            peer_group(0, 0, first=True)
            peer_group(1, 1)
            with pe.Fori(1, N_GROUPS // 2 - 1) as g2:
                peer_group(2 * g2, 0)
                peer_group(2 * g2 + 1, 1)
            peer_group(N_GROUPS - 2, 0)
            peer_group(N_GROUPS - 1, 1, last=True)

            pe.wait_ge(p_ready, 2)
            for n in range(DC):
                u, b = U_PROJ + n // 8, n % 8 * 2
                if n % 4 == 0:
                    half_in(u, n // 4 % 2)
                if n >= 2:
                    pe.wait_ge(dve_proj_out if n % 2 else act_proj_out, n // 2)
                for c in range(2):
                    mm = passes(bank[n % 2][:, :], b + c, u % 2, pt_hi[:, c, :], pt_lo[:, c, :], c == 0, c == 1)
                mm.then_inc(weights_used if n % 8 == 7 else proj_done, 1)
            pe.wait_ge(x3_ready, DC)
            pe.wait_ge(act_proj_out, DC // 2)
            pe.wait_ge(dve_proj_out, DC // 2)
            unit(U_GATE, U_GATE % 2, bank[0], x2_hi, x2_lo)
            pe.wait_ge(acc_step, 2 * ACC)
            pe.matmul(bank[7][:, :], ones[:, :], acc[:, :], start=True, stop=True).then_inc(stat_sum, 1)
            unit(U_GATE + 1, (U_GATE + 1) % 2, bank[1], x2_hi, x2_lo)
            with pe.Fori(1, DC // 2) as i:
                for k in range(2):
                    pe.wait_ge(gate_pre, 2 * i + k - 1)
                    unit(2 * i + k + U_GATE, (U_GATE + k) % 2, bank[k], x2_hi, x2_lo)
            pe.wait_ge(acc_step, 3 * ACC)
            pe.matmul(bank[7][:, :], ones[:, :], acc[:, :], start=True, stop=True).then_inc(stat_sum, 1)

        @block.scalar
        def _(act):
            def hi(u, slot, halves=(0, 1)):
                for s in halves:
                    act.wait_ge(raw_loaded[s], 16 * u + 16)
                    if s == 0 and not (isinstance(u, int) and u < 2):
                        act.wait_ge(weights_used, u - 1)
                    act.activation(w_hi[slot][:, 8 * s:8 * s + 8, :], raw[s][:, :, :], ACT.Copy)\
                       .then_inc(hi_ready, 1)

            def alone():
                act.wait_ge(small_in, 16)

            def std(k, buf):
                act.wait_ge(stat_var, k + 1)
                act.activation(buf[:, :], buf[:, :], ACT.Sqrt).then_inc(stat_std, 1)

            hi(0, 0)
            act.wait_ge(small_in, 16)
            for c in range(DC):
                if c % 4 == 0:
                    act.wait_ge(x_in[c // 4], 16)
                act.activation(x1_hi[:, c, :], h[:, c, :], ACT.Copy, scale=gain[:, c:c + 1]).then_inc(x1_hi_ready, 1)
                act.activation(sq_x[:, c, :], h[:, c, :], ACT.Square).then_inc(sq_ready, 1)
            hi(1, 1)
            std(0, rinv)
            act.wait_ge(rope_step, ROPE_STEPS)
            act.activation(table[:, :], ang[:, :], ACT.Sin).then_inc(rope_sin, 1)
            with act.Fori(0, 2) as i:
                hi(2 * i + 2, 0)
                hi(2 * i + 3, 1)

            def latent_sq(i):
                act.wait_ge(in_out, 4 * i + 4)
                act.activation(sq_l[:, :, :], z[:, 4 * i:4 * i + 4, :], ACT.Square).then_inc(lat_sq, 1)

            def latent_hi(i):
                for c in range(LC):
                    act.wait_ge(lat_norm, 4 * i + c + 1)
                    act.activation(l_hi[i][:, c, :], z[:, 4 * i + c, :], ACT.Copy).then_inc(lat_hi, 1)

            hi(6, 0)
            latent_sq(0)
            std(1, rinv_l)
            latent_hi(0)
            with act.Fori(0, 2) as i:
                hi(2 * i + 7, 1)
                hi(2 * i + 8, 0)
            latent_sq(1)
            hi(11, 1)
            std(2, rinv_l)
            latent_hi(1)
            hi(12, 0)
            act.wait_ge(key_sum, 1)
            act.activation(key_r[:, :], bank[6][:, :], ACT.Copy).then_inc(key_ready, 1)
            hi(13, 1)

            def head_qk(hd):
                act.wait_ge(q_done, hd + 1)
                act.activation(q_n[:, :], bank[0][:, :], ACT.Copy, scale=SCALE).then_inc(act_proj, 1)
                act.wait_ge(k_done, hd + 1)
                act.activation(k_n[:, :], bank[0][:, :], ACT.Copy).then_inc(act_proj, 1)

            def head_mixed(hd, y):
                for t in (1, 3):
                    act.wait_ge(turned, 4 * hd + t + 1)
                    act.activation(prob_t[:, 0:t + 1, t * P:(t + 1) * P],
                                   bank[7][:, 0:(t + 1) * P].rearrange("p (c q) -> p c q", q=P), ACT.Copy)\
                       .then_inc(act_turned, 1)
                alone()
                act.wait_ge(mixed, hd + 1)
                act.activation(y, bank[5][:, :], ACT.Copy).then_inc(y_hi, 1)

            def head_exp(hd):
                for t in range(TC):
                    lo, n = t * (t + 1) // 2, t + 1
                    act.wait_ge(neg_ready, 4 * hd + t + 1)
                    act.activation(prob[:, lo:lo + n, :].rearrange("p c k -> p (c k)"), bank[2 + t][:, 0:n * P],
                                   ACT.Exp, bias=neg_max[:, t:t + 1], accum_out=row_sum[:, t:t + 1])\
                       .then_inc(exp_ready, 1)

            hi(U_HEAD + 1, 0)
            head_qk(0)
            head_exp(0)
            for g in range(4):
                act.wait_ge(pool_mixed, g + 1)
                act.activation(x1_hi[:, g, :], bank[6 + g % 2][:, :], ACT.Copy,
                               scale=gain[:, G_POOL - C_GAIN + g:G_POOL - C_GAIN + g + 1]).then_inc(pool_hi, 1)
            with act.Fori(0, (HEADS - 2) // 2) as i:
                for k in range(2):
                    hd = 2 * i + 1 + k
                    hi(hd + U_HEAD + 1, (U_HEAD + 2 + k) % 2)
                    head_qk(hd)
                    head_mixed(hd - 1, x1_hi[:, bass.ds(4 + hd - 1, 1), :].rearrange("p a t -> p (a t)"))
                    head_exp(hd)
            hi(U_HEAD + HEADS, (U_HEAD + HEADS) % 2)
            head_qk(HEADS - 1)
            head_mixed(HEADS - 2, x1_hi[:, 4 + HEADS - 2, :])
            head_exp(HEADS - 1)
            head_mixed(HEADS - 1, x1_hi[:, 4 + HEADS - 1, :])

            def residual_out(n, k):
                hi(n + U_WO + 1, (U_WO + 1 + k) % 2)
                alone()
                act.wait_ge(h_ready, n + 1)
                act.activation(chunk(x2_hi, n), chunk(h, n), ACT.Copy, scale=gain[:, bass.ds(n + G_FFN - C_GAIN, 1)])\
                   .then_inc(x2_hi_ready, 1)
                if not isinstance(n, int):
                    alone()
                    act.wait_ge(acc_step, n)
                act.activation(bank[2 + k][:, :], chunk(h, n), ACT.Square).then_inc(h_sq, 1)

            residual_out(0, 0)
            residual_out(1, 1)
            with act.Fori(1, DC // 2) as i:
                for k in range(2):
                    residual_out(2 * i + k, k)

            def score_out(n, k):
                act.wait_ge(s_done, n + 1)
                act.activation(s_f[k][:, :, :].rearrange("p t n -> p (t n)"), bank[2 + k][:, :], ACT.Copy)\
                   .then_inc(s_ready, 1)

            def gates(hd):
                act.wait_ge(gate_in, hd + 1)
                act.activation(b_exp[:, :, :], b_exp[:, :, :], ACT.Exp).then_inc(gate_exp, 1)

            hi(U_WQ + 1, (U_WQ + 1) % 2)
            std(3, rinv)
            hi(U_WQ + 2, (U_WQ + 2) % 2)
            score_out(0, 0)
            with act.Fori(1, PH) as i:
                hi(2 * i + U_WQ + 1, (U_WQ + 1) % 2)
                score_out(2 * i - 1, 1)
                hi(2 * i + U_WQ + 2, (U_WQ + 2) % 2)
                gates(i - 1)
                score_out(2 * i, 0)
            score_out(2 * PH - 1, 1)
            gates(PH - 1)

            for i in range(3):
                act.wait_ge(hk_turned, i + 1)
                act.activation(hk_t[i][:, :], bank[2 + i][:, :], ACT.Copy).then_inc(hk_ready, 1)
            def g_evict(blk2, s, q):
                for half in range(2):
                    act.wait_ge(g_done, 2 * ((TB // OH) * (2 * blk2 + s) + q) + half + 1)
                    t0 = OH * q + 4 * half
                    act.activation(g_blk[s][:, :, t0:t0 + 4].rearrange("p i t -> p t i"),
                                   bank[6 + half][:, :].rearrange("p (t i) -> p t i", i=NK), ACT.Copy)\
                       .then_inc(g_out, 1)

            for s in range(2):
                for q in range(TB // OH):
                    g_evict(0, s, q)
            with act.Fori(1, N_TB // 2) as b2:
                for s in range(2):
                    act.wait_ge(g_stored[s], 16 * b2)
                    for q in range(TB // OH):
                        g_evict(b2, s, q)

            def activate(j, a):
                act.wait_ge(e_scaled, j + 1)
                act.activation(h_g[:, :], h_s[:, :], ACT.Gelu_apprx_tanh).then_inc(e_gelu, 1)
                act.wait_ge(e_gated, j + 1)
                act.activation(a_hi[a][:, :], h_a[:, :], ACT.Copy).then_inc(e_hi, 1)

            def third_hi(c):
                act.wait_ge(v_added, 16 * (N_GROUPS - 1) + c + 1)
                act.activation(x2_hi[:, c, :], h[:, c, :], ACT.Copy,
                               scale=gain[:, G_PLE - C_GAIN + c:G_PLE - C_GAIN + c + 1]).then_inc(x3_hi_ready, 1)
                if c >= 2:
                    act.wait_ge(acc_step, ACC + c)
                act.activation(bank[6 + c % 2][:, :], h[:, c, :], ACT.Square).then_inc(h3_sq, 1)

            def peer_group(g, par, last=False):
                for m in range(1, GROUP):
                    hi(peer_unit(g, m), peer_slot(m))
                    activate(g * GROUP + m, a_slot(m, par))
                if not last:
                    hi(peer_unit(g, 4), peer_slot(4))
                    activate((g + 1) * GROUP, a_slot(0, 1 - par))
                for q in range(4):
                    k = 5 + q - (1 if last else 0)
                    hi(peer_unit(g, k), peer_slot(k))
                    if last:
                        for c in range(4 * q, 4 * q + 4):
                            third_hi(c)

            for s in range(2):
                act.wait_ge(g_stored[s], 16 * (N_TB // 2))
            act.wait_ge(p_in, 16)
            for c in range(2):
                act.activation(pt_hi[:, c, :], pt[:, c, :], ACT.Copy).then_inc(p_hi, 1)
            hi(U_PEER + 1, peer_slot(0))
            activate(0, a_slot(0, 0))
            with act.Fori(0, N_GROUPS // 2 - 1) as g2:
                peer_group(2 * g2, 0)
                peer_group(2 * g2 + 1, 1)
            peer_group(N_GROUPS - 2, 0)
            peer_group(N_GROUPS - 1, 1, last=True)

            hi(U_PROJ + 1, (U_PROJ + 1) % 2)
            for n in range(0, DC, 2):
                if n == 8:
                    hi(U_GATE, U_GATE % 2)
                act.wait_ge(proj_done, n + 1 - n // 8)
                act.activation(proj[:, n, :], bank[0][:, :], ACT.Copy).then_inc(act_proj_out, 1)
            hi(U_GATE + 1, (U_GATE + 1) % 2)
            std(4, rinv)

            def gate_out(n, k, more=True):
                if more:
                    hi(n + U_GATE + 1, (U_GATE + 1 + k) % 2)
                act.wait_ge(gate_pre, n + 1)
                act.activation(g_sig[:, :], g_pre[:, :], ACT.Sigmoid).then_inc(gate_sig, 1)
                alone()
                act.wait_ge(h_end, n + 1)
                act.activation(bank[2 + k][:, :], chunk(h, n), ACT.Square).then_inc(end_sq, 1)

            act.wait_ge(gate_pre, 1)
            act.activation(g_sig[:, :], g_pre[:, :], ACT.Sigmoid).then_inc(gate_sig, 1)
            act.wait_ge(h_end, 1)
            act.activation(bank[2][:, :], h[:, 0, :], ACT.Square).then_inc(end_sq, 1)
            with act.Fori(0, (DC - 2) // 2) as i:
                gate_out(2 * i + 1, 1)
                gate_out(2 * i + 2, 0)
            gate_out(DC - 1, 1, more=False)
            std(5, rinv)

        @block.vector
        def _(dve):
            def lo(u, slot, halves=(0, 1)):
                for s in halves:
                    dve.wait_ge(hi_ready, 2 * u + s + 1)
                    dve.tensor_tensor(w_lo[slot][:, 8 * s:8 * s + 8, :], raw[s][:, :, :],
                                      w_hi[slot][:, 8 * s:8 * s + 8, :].bitcast(F32), ALU.subtract)\
                       .then_inc(lo_ready, 1)

            def inverse(k, buf, n):
                dve.wait_ge(stat_sum, k + 1)
                dve.tensor_scalar(buf[:, :], bank[7][:, :], 1.0 / n, EPS, ALU.mult, ALU.add).then_inc(stat_var, 1)
                dve.wait_ge(stat_std, k + 1)
                dve.reciprocal(buf[:, :], buf[:, :]).then_inc(stat_inv, 1)
                dve.wait_ge(stat_inv, k + 1)

            dve.wait_ge(const_in, 16 * 8)
            dve.tensor_copy(ident_b[:, :], ident[:, :]).then_inc(consts_done, 1)
            dve.tensor_copy(mask_b[:, :], mask_f[:, :]).then_inc(consts_done, 1)
            dve.memset(ones[:, :], 1.0).then_inc(consts_done, 1)
            rope = [0]

            def rope_do(ins):
                rope[0] += 1
                ins.then_inc(rope_step, 1)
                dve.wait_ge(rope_step, rope[0])

            two_pi = 2 * np.pi
            c1 = 6.28125
            c2 = float(np.float32(round((two_pi - c1) * 2 ** 21) / 2 ** 21))
            c3 = float(np.float32(two_pi - c1 - c2))
            magic = 1.5 * 2 ** 23
            rope_do(dve.tensor_copy(ang[:, :], pos_i[:, :]))
            rope_do(dve.tensor_scalar(ang[:, :], ang[:, :], rope_c[:, 0:1], None, ALU.mult))
            rope_do(dve.tensor_scalar(turn[:, :], ang[:, :], 1 / two_pi, magic, ALU.mult, ALU.add))
            rope_do(dve.tensor_scalar(turn[:, :], turn[:, :], -magic, None, ALU.add))
            for c in (c1, c2, c3):
                rope_do(dve.scalar_tensor_tensor(ang[:, :], turn[:, :], -c, ang[:, :], ALU.mult, ALU.add))
            rope_do(dve.tensor_scalar(ang[:, :], ang[:, :], rope_c[:, 1:2], None, ALU.add))
            rope_do(dve.tensor_scalar(turn[:, :], ang[:, :], float(np.float32(np.pi)), -two_pi, ALU.is_gt, ALU.mult))
            rope_do(dve.tensor_tensor(ang[:, :], ang[:, :], turn[:, :], ALU.add))
            rope_do(dve.tensor_scalar(ang[:, :], ang[:, :], 3.1415925, -3.1415925, ALU.min, ALU.max))
            assert rope[0] == ROPE_STEPS

            lo(0, 0)
            for c in range(DC):
                dve.wait_ge(x1_hi_ready, c + 1)
                dve.scalar_tensor_tensor(x1_lo[:, c, :], h[:, c, :], gain[:, c:c + 1],
                                         x1_hi[:, c, :].bitcast(F32), ALU.mult, ALU.subtract).then_inc(x1_ready, 1)
            lo(1, 1)
            inverse(0, rinv, D)

            def in_evict(u, slot):
                dve.wait_ge(weights_used, u + 1)
                dve.tensor_tensor(chunk(z, u), bank[slot][:, :], rinv[:, :], ALU.mult).then_inc(in_out, 1)

            def latent(i):
                inverse(i + 1, rinv_l, LC * P)
                for c in range(LC):
                    zc = z[:, 4 * i + c, :]
                    dve.scalar_tensor_tensor(zc, zc, gain[:, G_Q - C_GAIN + 4 * i + c:G_Q - C_GAIN + 4 * i + c + 1],
                                             rinv_l[:, :], ALU.mult, ALU.mult).then_inc(lat_norm, 1)
                for c in range(LC):
                    dve.wait_ge(lat_hi, 4 * i + c + 1)
                    dve.tensor_tensor(l_lo[i][:, c, :], z[:, 4 * i + c, :], l_hi[i][:, c, :].bitcast(F32),
                                      ALU.subtract).then_inc(lat_ready, 1)

            in_evict(0, 0)
            with dve.Fori(0, 2) as i:
                lo(2 * i + 2, 0)
                in_evict(2 * i + 1, 1)
                lo(2 * i + 3, 1)
                in_evict(2 * i + 2, 0)
            lo(6, 0)
            in_evict(5, 1)
            latent(0)
            with dve.Fori(0, 2) as i:
                lo(2 * i + 7, 1)
                in_evict(2 * i + 6, 0)
                lo(2 * i + 8, 0)
                in_evict(2 * i + 7, 1)
            dve.wait_ge(in_out, 9)
            dve.wait_ge(rope_sin, 1)
            dve.tensor_tensor(key_p[:, :], z[:, 8, :], table[:, :], ALU.mult).then_inc(key_turned, 1)
            lo(11, 1)
            latent(1)
            in_evict(10, 0)
            lo(12, 0)
            in_evict(11, 1)
            lo(13, 1)
            in_evict(12, 0)

            def head_rv(hd):
                dve.wait_ge(r_done, hd + 1)
                dve.scalar_tensor_tensor(q_r[:, :], bank[1][:, :], SCALE, table[:, :], ALU.mult, ALU.mult)\
                   .then_inc(dve_proj, 1)

            def head_v(hd, par):
                dve.wait_ge(weights_used, U_HEAD + hd + 1)
                dve.tensor_copy(v_h[par][:, :, :].rearrange("p c d -> p (c d)"), bank[1][:, :]).then_inc(dve_proj, 1)

            def head_mixed(hd, n):
                for t in (0, 2):
                    dve.wait_ge(turned, 4 * hd + t + 1)
                    dve.tensor_copy(prob_t[:, 0:t + 1, t * P:(t + 1) * P],
                                    bank[6][:, 0:(t + 1) * P].rearrange("p (c q) -> p c q", q=P)).then_inc(dve_turned, 1)
                dve.wait_ge(y_hi, hd + 1)
                dve.tensor_tensor(chunk(x1_lo, n), bank[5][:, :], chunk(x1_hi, n).bitcast(F32), ALU.subtract)\
                   .then_inc(y_ready, 1)

            def head_softmax(hd):
                for t in range(TC):
                    dve.wait_ge(scores_done, 4 * hd + t + 1)
                    dve.tensor_reduce(neg_max[:, t:t + 1], bank[2 + t][:, 0:(t + 1) * P], AX.X, ALU.max, negate=True)\
                       .then_inc(neg_ready, 1)
                dve.wait_ge(exp_ready, 4 * hd + 4)
                dve.reciprocal(row_inv[:, :], row_sum[:, :]).then_inc(sum_inv, 1)
                dve.wait_ge(sum_inv, hd + 1)
                for t in range(TC):
                    a = t * (t + 1) // 2
                    pt_ = prob[:, a:a + t + 1, :]
                    dve.tensor_scalar(pt_, pt_, row_inv[:, t:t + 1], None, ALU.mult).then_inc(prob_ready, 1)

            lo(U_HEAD + 1, (U_HEAD + 1) % 2)
            head_rv(0)
            head_v(0, 0)
            head_softmax(0)
            for g in range(4):
                dve.wait_ge(pool_hi, g + 1)
                dve.scalar_tensor_tensor(x1_lo[:, g, :], bank[6 + g % 2][:, :],
                                         gain[:, G_POOL - C_GAIN + g:G_POOL - C_GAIN + g + 1],
                                         x1_hi[:, g, :].bitcast(F32), ALU.mult, ALU.subtract).then_inc(pool_ready, 1)

            def head(hd, k):
                lo(hd + U_HEAD + 1, (U_HEAD + 1 + k) % 2)
                head_rv(hd)
                head_v(hd, k % 2)
                head_mixed(hd - 1, hd + 3)
                head_softmax(hd)

            with dve.Fori(0, (HEADS - 2) // 2) as i:
                head(2 * i + 1, 1)
                head(2 * i + 2, 2)
            head(HEADS - 1, HEADS - 1)
            head_mixed(HEADS - 1, HEADS + 3)

            def acc_clear(a):
                dve.memset(acc[:, :], 0.0).then_inc(acc_step, 1)

            def acc_add(a, n, b, squares):
                dve.wait_ge(squares, n + 1)
                dve.wait_ge(acc_step, ACC * a + n + 1)
                dve.tensor_tensor(acc[:, :], acc[:, :], bank[b][:, :], ALU.add).then_inc(acc_step, 1)

            acc_clear(0)
            dve.wait_ge(x_again, 64)
            with dve.Fori(0, DC // 2) as i:
                for k in range(2):
                    n = 2 * i + k
                    lo(n + U_WO + 1, (U_WO + 1 + k) % 2)
                    dve.wait_ge(weights_used, n + U_WO + 1)
                    dve.tensor_tensor(chunk(h, n), bank[k][:, :], chunk(h, n), ALU.add).then_inc(h_ready, 1)
                    dve.wait_ge(x2_hi_ready, n + 1)
                    dve.scalar_tensor_tensor(chunk(x2_lo, n), chunk(h, n), gain[:, bass.ds(n + G_FFN - C_GAIN, 1)],
                                             chunk(x2_hi, n).bitcast(F32), ALU.mult, ALU.subtract)\
                       .then_inc(x2_ready, 1)
                    acc_add(0, n, 2 + k, h_sq)

            def before_max(semaphore, value):
                dve.wait_ge(semaphore, value)
                dve.tensor_copy(carrier[:, :], iota[:, 0:1])

            def step_by_step(done):
                k = [0]

                def step(ins, max_next=False):
                    k[0] += 1
                    ins.then_inc(topk_step, 1)
                    if max_next:
                        before_max(topk_step, done + k[0])
                    else:
                        dve.wait_ge(topk_step, done + k[0])
                return step, k

            def query_out(n, k):
                dve.wait_ge(weights_used, n + U_WQ + 1)
                dve.tensor_tensor(q_f[k][:, :], bank[k][:, :], rinv[:, :], ALU.mult).then_inc(q_ready, 1)

            LOWEST = -3.0e38

            def top16(step, values, index, src, cut, n):
                for t in range(TC):
                    ins = dve.max(values[:, t, 0:8], src[:, t, 0:n])
                step(ins, max_next=True)
                for t in range(TC):
                    dve.max_index(index[:, t, 0:8], values[:, t, 0:8], src[:, t, 0:n])
                    ins = dve.match_replace(cut[:, t, 0:n], values[:, t, 0:8], src[:, t, 0:n], LOWEST)
                step(ins, max_next=True)
                for t in range(TC):
                    ins = dve.max(values[:, t, 8:16], cut[:, t, 0:n])
                step(ins, max_next=True)
                for t in range(TC):
                    ins = dve.max_index(index[:, t, 8:16], values[:, t, 8:16], cut[:, t, 0:n])
                step(ins)

            def half_topk(step, n, p):
                before_max(s_ready, n + 1)
                top16(step, t_v[p], t_i[p], s_f[p], s_cut, NK)
                step(dve.tensor_copy(t_if[p][:, :, :], t_i[p][:, :, :]))

            def pair_topk(step, hd):
                step(dve.tensor_tensor(cand[:, :, :, :],
                                       t_v[0][:, :, :].unsqueeze(3).to_broadcast([P, TC, TOPK, TOPK]),
                                       t_v[1][:, :, :].unsqueeze(2).to_broadcast([P, TC, TOPK, TOPK]), ALU.add),
                     max_next=True)
                top16(step, b_v, b_pos, cand[:, :, :, :].rearrange("p t a b -> p t (a b)"), cand_cut, TOPK * TOPK)
                dve.tensor_tensor(b_exp[:, :, :], b_v[:, :, :], b_v[:, :, 0:1].to_broadcast([P, TC, TOPK]),
                                  ALU.subtract).then_inc(gate_in, 1)
                flat = b_pos[:, :, :].rearrange("p t k -> p (t k)")
                dve.tensor_scalar(pos_hl[0][:, :], flat, 4, None, ALU.logical_shift_right)
                step(dve.tensor_scalar(pos_hl[1][:, :], flat, 15, None, ALU.bitwise_and))
                for p in range(2):
                    dve.tensor_tensor(pick[p][:, :, :], pos_hl[p][:, :].unsqueeze(2).to_broadcast([P, TC * TOPK, TOPK]),
                                      iota[:, None, 0:TOPK].to_broadcast([P, TC * TOPK, TOPK]), ALU.is_equal)\
                       .then_inc(pick_ready, 1)
                dve.wait_ge(gate_exp, hd + 1)
                step(dve.tensor_reduce(b_sum[:, :], b_exp[:, :, :], AX.X, ALU.add))
                step(dve.reciprocal(b_inv[:, :], b_sum[:, :]))

                def chosen(i):
                    if isinstance(hd, int):
                        return sel[i][:, :, hd, :]
                    return sel[i][:, :, bass.ds(hd, 1), :].rearrange("p t a k -> p t (a k)")

                step(dve.tensor_tensor(chosen(2), b_exp[:, :, :], b_inv[:, :].unsqueeze(2).to_broadcast([P, TC, TOPK]),
                                       ALU.mult))
                dve.wait_ge(picked_ready, 2 * hd + 2)
                for p in range(2):
                    ins = dve.tensor_reduce(chosen(p), picked[p][:, :, :].rearrange("p (t k) m -> p t k m", t=TC),
                                            AX.X, ALU.add)
                step(ins)

            def topk_head(hd, between=None):
                step, k = step_by_step(PER_TOPK * hd)
                half_topk(step, 2 * hd, 0)
                if between:
                    between()
                half_topk(step, 2 * hd + 1, 1)
                pair_topk(step, hd)
                assert k[0] == PER_TOPK

            lo(U_WQ + 1, (U_WQ + 1) % 2)
            inverse(3, rinv, D)
            query_out(0, 0)
            lo(U_WQ + 2, (U_WQ + 2) % 2)
            query_out(1, 1)
            with dve.Fori(1, PH) as i:
                lo(2 * i + U_WQ + 1, (U_WQ + 1) % 2)

                def next_query():
                    query_out(2 * i, 0)
                    lo(2 * i + U_WQ + 2, (U_WQ + 2) % 2)

                topk_head(i - 1, next_query)
                query_out(2 * i + 1, 1)
            topk_head(PH - 1)

            def one_hots(q, s, first=False):
                o = [P, OH, NK]
                if not first:
                    dve.wait_ge(oh_g, q - 1)
                dve.tensor_tensor(one_i[s][:, :, :], iota[:, None, :].to_broadcast(o),
                                  hk_t[0][:, bass.ds(OH * q, OH)].unsqueeze(2).to_broadcast(o), ALU.is_equal)\
                   .then_inc(oh_i, 1)
                if not first:
                    dve.wait_ge(g_done, 2 * q - 2)
                dve.tensor_tensor(one_j[s][:, :, :], iota[:, None, :].to_broadcast(o),
                                  hk_t[1][:, bass.ds(OH * q, OH)].unsqueeze(2).to_broadcast(o), ALU.is_equal)\
                   .then_inc(oh_j, 1)

            dve.wait_ge(hk_ready, 3)
            one_hots(0, 0, first=True)
            one_hots(1, 1, first=True)
            with dve.Fori(1, T // OH // 2) as q2:
                for s in range(2):
                    one_hots(2 * q2 + s, s)

            def activated(j, m, n_tile, b, a):
                par, n = n_tile
                dve.wait_ge(weights_used, n_unit[0] + 1)
                dve.tensor_tensor(h_s[:, :], bank[b][:, :], rinv[:, :], ALU.mult).then_inc(e_scaled, 1)
                dve.wait_ge(e_gelu, j + 1)
                dve.wait_ge(g_in[par], 16 * n + 16)
                dve.tensor_tensor(h_a[:, :].rearrange("p (b t) -> p b t", t=TB),
                                  h_g[:, :].rearrange("p (b t) -> p b t", t=TB), g_tile[par][:, :, m, :], ALU.mult)\
                   .then_inc(e_gated, 1)
                dve.wait_ge(e_hi, j + 1)
                dve.tensor_tensor(a_lo[a][:, :], h_a[:, :], a_hi[a][:, :].bitcast(F32), ALU.subtract)\
                   .then_inc(e_ready, 1)

            n_unit = [0]

            def peer_group(g, g2, par, last=False):
                for m in range(1, GROUP):
                    lo(peer_unit(g, m), peer_slot(m))
                    n_unit[0] = peer_unit(g, m - 1)
                    activated(g * GROUP + m, m, (par, g2), m % 2, a_slot(m, par))
                if not last:
                    lo(peer_unit(g, 4), peer_slot(4))
                    n_unit[0] = peer_unit(g, 3)
                    activated((g + 1) * GROUP, 0, (1 - par, g2 + par), 0, a_slot(0, 1 - par))
                for q in range(4):
                    k = 4 + q - (1 if last else 0)
                    lo(peer_unit(g, k + 1), peer_slot(k + 1), halves=(0,))
                    for c in range(4):
                        if c < 3:
                            dve.wait_ge(v_done, 12 * g + 3 * q + c + 1)
                        else:
                            dve.wait_ge(weights_used, peer_unit(g, k) + 1)
                        hc = h[:, 4 * q + c, :]
                        dve.tensor_tensor(hc, bank[2 + c][:, :], hc, ALU.add).then_inc(v_added, 1)
                        if c == 0:
                            lo(peer_unit(g, k + 1), peer_slot(k + 1), halves=(1,))
                    if last:
                        for c in range(4 * q, 4 * q + 4):
                            third_lo(c)

            def third_lo(c):
                dve.wait_ge(x3_hi_ready, c + 1)
                dve.scalar_tensor_tensor(x2_lo[:, c, :], h[:, c, :],
                                         gain[:, G_PLE - C_GAIN + c:G_PLE - C_GAIN + c + 1],
                                         x2_hi[:, c, :].bitcast(F32), ALU.mult, ALU.subtract).then_inc(x3_ready, 1)
                acc_add(1, c, 6 + c % 2, h3_sq)

            for s in range(2):
                dve.wait_ge(g_stored[s], 16 * (N_TB // 2))
            for c in range(2):
                dve.wait_ge(p_hi, c + 1)
                dve.tensor_tensor(pt_lo[:, c, :], pt[:, c, :], pt_hi[:, c, :].bitcast(F32), ALU.subtract)\
                   .then_inc(p_ready, 1)
            acc_clear(1)
            lo(U_PEER + 1, peer_slot(0))
            n_unit[0] = U_PEER
            activated(0, 0, (0, 0), 0, a_slot(0, 0))
            with dve.Fori(0, N_GROUPS // 2 - 1) as g2:
                peer_group(2 * g2, g2, 0)
                peer_group(2 * g2 + 1, g2, 1)
            peer_group(N_GROUPS - 2, N_GROUPS // 2 - 1, 0)
            peer_group(N_GROUPS - 1, N_GROUPS // 2 - 1, 1, last=True)

            lo(U_PROJ + 1, (U_PROJ + 1) % 2)
            for n in range(1, DC, 2):
                if n == 9:
                    lo(U_GATE, U_GATE % 2)
                if n % 8 == 7:
                    dve.wait_ge(weights_used, U_PROJ + n // 8 + 1)
                else:
                    dve.wait_ge(proj_done, n + 1 - n // 8)
                dve.tensor_copy(proj[:, n, :], bank[1][:, :]).then_inc(dve_proj_out, 1)
            lo(U_GATE + 1, (U_GATE + 1) % 2)
            inverse(4, rinv, D)
            acc_clear(2)

            def gate_out(n, k, more=True):
                if more:
                    lo(n + U_GATE + 1, (U_GATE + 1 + k) % 2)
                dve.wait_ge(weights_used, n + U_GATE + 1)
                dve.tensor_tensor(g_pre[:, :], bank[k][:, :], rinv[:, :], ALU.mult).then_inc(gate_pre, 1)
                dve.wait_ge(gate_sig, n + 1)
                dve.tensor_tensor(g_mul[:, :], g_sig[:, :], chunk(proj, n), ALU.mult).then_inc(gate_mul, 1)
                dve.wait_ge(gate_mul, n + 1)
                dve.tensor_tensor(chunk(h, n), chunk(h, n), g_mul[:, :], ALU.add).then_inc(h_end, 1)
                acc_add(2, n, 2 + k, end_sq)

            gate_out(0, 0, more=False)
            with dve.Fori(0, (DC - 2) // 2) as i:
                gate_out(2 * i + 1, 1)
                gate_out(2 * i + 2, 0)
            gate_out(DC - 1, 1, more=False)
            inverse(5, rinv, D)
            for c in range(DC):
                dve.scalar_tensor_tensor(proj[:, c, :], h[:, c, :],
                                         gain[:, G_FIN - C_GAIN + c:G_FIN - C_GAIN + c + 1], rinv[:, :],
                                         ALU.mult, ALU.mult).then_inc(fin_ready, 1)

        @block.gpsimd
        def _(pool):
            for c in range(1, DC):
                pool.wait_ge(sq_ready, c + 1)
                if c > 1:
                    pool.wait_ge(pool_step, c - 1)
                pool.tensor_tensor(x_acc[:, :], sq_x[:, 0, :] if c == 1 else x_acc[:, :], sq_x[:, c, :], ALU.add)\
                    .then_inc(pool_step, 1)

            steps = [0]

            def win_do(ins):
                steps[0] += 1
                ins.then_inc(win_step, 1)
                pool.wait_ge(win_step, steps[0])

            for g, w in enumerate(WINDOWS):
                if g:
                    pool.wait_ge(pooled, g)
                pool.wait_ge(in_out, 10 + g)
                src, i = z[:, 9 + g, :], 0
                for e in range(g + 1):
                    s = 2 ** e
                    win_do(pool.tensor_tensor(win[i][:, s:T], src[:, s:T], src[:, 0:T - s], ALU.add))
                    win_do(pool.tensor_copy(win[i][:, 0:s], src[:, 0:s]))
                    src, i = win[i][:, :], 1 - i
                win_do(pool.tensor_scalar(win[i][:, w:T], src[:, w:T], 1.0 / w, None, ALU.mult))
                win_do(pool.tensor_tensor(win[i][:, 0:w], src[:, 0:w], p_inv[:, g, 0:w], ALU.mult))
                pool.tensor_tensor(z[:, 9 + g, :], win[i][:, :], z[:, 9 + g, :], ALU.subtract).then_inc(pooled, 1)

            with pool.Fori(0, PH) as hd:
                for p in range(2):
                    pool.wait_ge(pick_ready, 2 * hd + p + 1)
                    pool.tensor_tensor(
                        picked[p][:, :, :].rearrange("p (t k) m -> p t k m", t=TC),
                        pick[p][:, :, :].rearrange("p (t k) m -> p t k m", t=TC),
                        t_if[p][:, :, :].unsqueeze(2).to_broadcast([P, TC, TOPK, TOPK]), ALU.mult)\
                        .then_inc(picked_ready, 1)

            def gated(q, s, first=False):
                pool.wait_ge(oh_i, q + 1)
                if not first:
                    pool.wait_ge(g_done, 2 * q - 2)
                pool.tensor_tensor(one_g[s][:, :, :], one_i[s][:, :, :],
                                   hk_t[2][:, bass.ds(OH * q, OH)].unsqueeze(2).to_broadcast([P, OH, NK]), ALU.mult)\
                    .then_inc(oh_g, 1)

            gated(0, 0, first=True)
            gated(1, 1, first=True)
            with pool.Fori(1, T // OH // 2) as q2:
                for s in range(2):
                    gated(2 * q2 + s, s)


def _units(w, rows, cols):
    return np.ascontiguousarray(w.reshape(rows, P, cols, P).transpose(2, 1, 0, 3))


def _columns(g):
    return np.asarray(g).reshape(-1, P).T


def _constants():
    c = np.zeros((P, 4 * P), np.float32)
    r = np.arange(P)
    c[:, C_IDENT:C_IDENT + P] = np.eye(P)
    c[:, C_IOTA:C_IOTA + P] = r
    c[:, C_MASK:C_MASK + P] = np.where(r[None, :] <= r[:, None], 0.0, -1e30)
    c[:, C_DUP:C_DUP + P] = (r[:, None] % 64 == r[None, :] % 64)
    return c


def _rope_columns():
    freq = np.float32(10000.0) ** (-np.arange(0, 64, 2, dtype=np.float32) / np.float32(64))
    phase = np.repeat(np.array([np.pi / 2, np.pi / 2, np.pi, 0.0]), 32)
    return np.stack([np.tile(freq, 4), phase], 1).astype(np.float32)


def _pool_inverse():
    t = np.arange(16)
    return np.broadcast_to(np.stack([1.0 / np.minimum(t + 1, w) for w in WINDOWS])[None], (P, 4, 16)).astype(np.float32)


def kernel(x, p, positions, mix_norm_g, w_in, pool_w, pool_scale, q_norm_g, w_uq, kv_norm_g, w_ukv, w_o,
           ffn_norm_g, peer_wq, peer_sub_keys, peer_u, peer_v, ple_norm_g, ple_w_gate, ple_w_proj, final_norm_g):
    import concourse.bacc as bacc
    from concourse.bass_utils import run_bass_kernel_spmd

    a = np.asarray
    turn = np.r_[0:32, 32:64, 32:64, 0:32]
    w = a(w_in)[0]
    w = np.concatenate([w[:, 512:1536], w[:, 1536:1600][:, turn], w[:, 0:512]], 1)
    uq = a(w_uq)[0].reshape(LC, P, HEADS, QK)
    ukv = a(w_ukv)[0].reshape(LC, P, HEADS, 2 * P)
    head = np.concatenate([uq[..., :P], uq[..., P:][..., turn], ukv[..., :P], ukv[..., P:]], 0)
    arrays = {
        "x_t": a(x)[0].T.reshape(DC, P, T).transpose(1, 0, 2),
        "p_t": a(p)[0, 0].T.reshape(2, P, T).transpose(1, 0, 2),
        "positions": a(positions),
        "gains": np.concatenate([_columns(g) for g in (mix_norm_g, ffn_norm_g, ple_norm_g, final_norm_g, q_norm_g,
                                                       kv_norm_g, pool_scale)], 1),
        "consts": _constants(),
        "rope_cols": _rope_columns(),
        "pool_inv": _pool_inverse(),
        "w_in": _units(w, DC, N_IN),
        "pool_w": a(pool_w)[0].transpose(1, 0, 2),
        "w_head": head.transpose(2, 1, 0, 3),
        "w_o": _units(a(w_o)[0], DC, DC),
        "w_q": _units(a(peer_wq)[0], DC, DC),
        "keys": a(peer_sub_keys)[0].reshape(2 * PH, NK, P).transpose(2, 0, 1),
        "u_t": a(peer_u)[0].reshape(NK, NK, DC, P).transpose(0, 3, 2, 1),
        "v": a(peer_v)[0],
        "w_proj": a(ple_w_proj)[0].reshape(2, P, 2, 8, P).transpose(2, 1, 3, 0, 4).reshape(2, P, 16, P),
        "w_gate": _units(a(ple_w_gate)[0], DC, DC),
    }
    arrays = {n: np.ascontiguousarray(v) for n, v in arrays.items()}
    nc = bacc.Bacc("TRN2", target_bir_lowering=False, num_devices=1)
    aps = {n: nc.dram_tensor(f"in_{n}", v.shape, mybir.dt.from_np(v.dtype), kind="ExternalInput").ap()
           for n, v in arrays.items()}
    out = nc.dram_tensor("out_t", (P, DC, T), F32, kind="ExternalOutput").ap()
    build_block(nc, **aps, out_t=out)
    got = run_bass_kernel_spmd(nc, [{f"in_{n}": v for n, v in arrays.items()}], core_ids=[0])
    return got.results[0]["out_t"].transpose(2, 1, 0).reshape(1, T, D)
```

```python
from contextlib import ExitStack

import concourse.bass as bass
import numpy as np
from concourse import mybir

F32 = mybir.dt.float32
F32R = mybir.dt.float32r
BF16 = mybir.dt.bfloat16
U32 = mybir.dt.uint32
I32 = mybir.dt.int32
ALU = mybir.AluOpType
ACT = mybir.ActivationFunctionType
AX = mybir.AxisListType

P = 128
T = 512
D = 2048
DC = D // P
TC = T // P
EPS = 1e-6
HEADS = 12
LC = 512 // P
QK = 192
SCALE = QK ** -0.5
WINDOWS = (2, 4, 8, 16)
PH = 8
TOPK = 16
NK = 128
HK = PH * TOPK
D_PLE = 256

U_IN = 0
N_IN = 13
U_HEAD0 = U_IN + N_IN
HEAD_HALF = 6
U_V = U_HEAD0 + 1
N_V = HEADS // 4
U_HEAD = U_V + N_V - 1
U_WO = U_HEAD + HEADS
U_WQ = U_WO + DC
GROUP = 4
N_GROUPS = NK // GROUP
U_ALONE = U_WQ + 2 * PH + 2 * (PH - 1)
ALONE = 3
U_BLOCK = U_ALONE + ALONE
U_PEER = U_WQ + 2 * PH + N_GROUPS
PER_GROUP = 7
N_PEER = PER_GROUP * N_GROUPS
U_PROJ = U_PEER + N_PEER
U_GATE = U_PROJ + 2

C_IDENT, C_IOTA, C_MASK, C_DUP = 0, 128, 256, 384
C_GAIN = 512
G_MIX, G_FFN, G_PLE, G_FIN, G_Q, G_KV, G_POOL = (C_GAIN + o for o in (0, 16, 32, 48, 64, 68, 72))
N_GAIN = 76

TB = 32
N_TB = T // TB
OH = 8


def build_block(nc, x_t, p_t, positions, gains, consts, rope_cols, pool_inv, w_in, pool_w, w_head, w_v,
                w_o, w_q, keys, u_t, v, w_proj, w_gate, out_t):
    ctx = ExitStack()
    with ctx:
        base = (nc.sbuf_base + 63) // 64 * 64
        h_dram = nc.dram_tensor("spilled_scores", (N_GROUPS, P, T), F32, kind="Internal").ap()
        g_dram = nc.dram_tensor("gate_matrix", (N_TB, P, NK, TB), F32, kind="Internal").ap()

        def at(name, offset, shape, dtype=F32):
            return nc.alloc_sbuf_tensor_at(name, shape, dtype, offset=base + offset)

        K = 1024
        raw = [at(f"raw{s}", 4 * K * s, [P, 8, P]) for s in range(2)]
        w_hi = [at(f"w_hi{s}", (8 + 8 * s) * K, [P, 16, P], F32R) for s in range(2)]
        w_lo = [at(f"w_lo{s}", (24 + 8 * s) * K, [P, 16, P], F32R) for s in range(2)]
        h_at, one, two, rest = 40 * K, 72 * K, 136 * K, 200 * K
        h = at("h", h_at, [P, DC, T])
        x1_hi = at("x1_hi", one, [P, DC, T], F32R)
        v_all = at("v_all", one, [P, DC, T])
        x1_lo = at("x1_lo", one + 32 * K, [P, DC, T], F32R)
        x2_hi = at("x2_hi", two, [P, DC, T], F32R)
        x2_lo = at("x2_lo", two + 32 * K, [P, DC, T], F32R)
        ident = at("ident", rest, [P, P])
        iota = at("iota", rest + 512, [P, P])
        ones = at("ones", rest + K, [P, P])
        ident_b = at("ident_b", rest + K + 512, [P, P], BF16)
        mask_b = at("mask_b", rest + K + 768, [P, P], BF16)
        gain = at("gain", rest + 2 * K, [P, N_GAIN])
        rope_c = at("rope_c", rest + 2 * K + 320, [P, 2])
        p_inv = at("p_inv", rest + 2 * K + 352, [P, 4, 16])
        neg_max = at("neg_max", rest + 2 * K + 640, [P, TC])
        row_sum = at("row_sum", rest + 2 * K + 672, [P, TC])
        row_inv = at("row_inv", rest + 2 * K + 704, [P, TC])
        rinv = at("rinv", rest + 3 * K, [P, T])
        table = at("table", rest + 5 * K, [P, T])
        acc = table

        z = at("z", h_at, [P, N_IN, T])
        win = [at(f"win{i}", h_at + (26 + 2 * i) * K, [P, T]) for i in range(2)]
        sq_x = at("sq_x", two, [P, DC, T])
        x_acc = at("x_acc", two + 32 * K, [P, T])
        pos_i = at("pos_i", two + 34 * K, [P, T], I32)
        ang = at("ang", two + 36 * K, [P, T])
        turn = at("turn", two + 38 * K, [P, T])
        mask_f = at("mask_f", two + 44 * K, [P, P])
        l_hi = [at(f"l_hi{i}", two + 16 * K * i, [P, LC, T], F32R) for i in range(2)]
        l_lo = [at(f"l_lo{i}", two + 16 * K * i + 8 * K, [P, LC, T], F32R) for i in range(2)]
        sq_l = at("sq_l", two + 32 * K, [P, LC, T])
        rinv_l = at("rinv_l", two + 42 * K, [P, T])
        q_n = at("q_n", two + 32 * K, [P, T])
        q_r = at("q_r", two + 34 * K, [P, T])
        k_n = at("k_n", two + 36 * K, [P, T])
        v_h = [at(f"v_h{i}", two + (38 + 2 * i) * K, [P, TC, P]) for i in range(2)]
        prob_t = at("prob_t", two + 42 * K, [P, TC, T])
        prob = at("prob", two + 50 * K, [P, TC * (TC + 1) // 2, P])
        key_p = at("key_p", two + 55 * K, [P, T])
        key_r = at("key_r", two + 57 * K, [P, T])
        pool_wt = at("pool_wt", two + 59 * K, [P, 4, P])
        dup = at("dup", two + 61 * K, [P, P])

        k_all = at("k_all", one, [P, 2 * PH, NK])
        q_f = [at(f"q_f{i}", one + (8 + 2 * i) * K, [P, T]) for i in range(2)]
        s_f = [at(f"s_f{i}", one + (12 + 2 * i) * K, [P, TC, NK]) for i in range(2)]
        s_cut = at("s_cut", one + 16 * K, [P, TC, NK])
        carrier = at("carrier", one + 54 * K, [P, 1])
        cand = at("cand", one + 18 * K, [P, TC, TOPK, TOPK])
        cand_cut = at("cand_cut", one + 22 * K, [P, TC, TOPK * TOPK])
        pick = [at(f"pick{i}", one + (26 + 4 * i) * K, [P, TC * TOPK, TOPK]) for i in range(2)]
        picked = [at(f"picked{i}", one + (34 + 4 * i) * K, [P, TC * TOPK, TOPK]) for i in range(2)]
        sel = [at(f"sel{i}", one + (42 + 2 * i) * K, [P, TC, PH, TOPK]) for i in range(3)]
        t_v = [at(f"t_v{i}", one + 48 * K + 256 * i, [P, TC, TOPK]) for i in range(2)]
        t_i = [at(f"t_i{i}", one + 49 * K + 256 * i, [P, TC, TOPK], U32) for i in range(2)]
        b_v = at("b_v", one + 50 * K, [P, TC, TOPK])
        b_pos = at("b_pos", one + 50 * K + 256, [P, TC, TOPK], U32)
        pos_hl = [at(f"pos_hl{i}", one + 51 * K + 256 * i, [P, TC * TOPK], U32) for i in range(2)]
        b_exp = at("b_exp", one + 52 * K, [P, TC, TOPK])
        b_sum = at("b_sum", one + 52 * K + 256, [P, TC])
        b_inv = at("b_inv", one + 52 * K + 320, [P, TC])
        t_if = [at(f"t_if{i}", one + 53 * K + 256 * i, [P, TC, TOPK]) for i in range(2)]
        hk_t = [at(f"hk_t{i}", one + 2 * K * i, [P, T]) for i in range(3)]
        one_i = [at(f"one_i{i}", one + (6 + 4 * i) * K, [P, OH, NK]) for i in range(2)]
        one_g = [at(f"one_g{i}", one + (14 + 4 * i) * K, [P, OH, NK]) for i in range(2)]
        one_j = [at(f"one_j{i}", one + (22 + 4 * i) * K, [P, OH, NK]) for i in range(2)]
        g_blk = [at(f"g_blk{i}", one + (30 + 16 * i) * K, [P, NK, TB]) for i in range(2)]
        h_out = at("h_out", one + 62 * K, [P, T])
        a_hi = [at(f"a_hi{i}", one + 2 * K * i, [P, T], F32R) for i in range(5)]
        a_lo = [at(f"a_lo{i}", one + (10 + 2 * i) * K, [P, T], F32R) for i in range(5)]
        g_tile = [at(f"g_tile{i}", one + (20 + 8 * i) * K, [P, N_TB, GROUP, TB]) for i in range(2)]
        h_pre = [at(f"h_pre{i}", one + (56 + 2 * i) * K, [P, T]) for i in range(2)]
        h_s = at("h_s", one + 36 * K, [P, T])
        h_g = at("h_g", one + 38 * K, [P, T])
        h_a = at("h_a", one + 40 * K, [P, T])
        pt = at("pt", one + 44 * K, [P, 2, T])
        pt_hi = at("pt_hi", one + 48 * K, [P, 2, T], F32R)
        pt_lo = at("pt_lo", one + 52 * K, [P, 2, T], F32R)
        sq_h = [at(f"sq_h{i}", one + (60 + 2 * i) * K, [P, T]) for i in range(2)]
        proj = at("proj", one, [P, DC, T])
        g_pre = at("g_pre", one + 56 * K, [P, T])
        g_sig = at("g_sig", one + 58 * K, [P, T])
        g_mul = at("g_mul", one + 60 * K, [P, T])

        bank = [ctx.enter_context(nc.psum_tensor(f"bank{i}", [P, T], F32)) for i in range(8)]

        def sem(name):
            return ctx.enter_context(nc.semaphore(name))

        raw_loaded = [sem(f"raw_loaded{s}") for s in range(2)]
        hi_ready = sem("hi_ready")
        lo_ready = sem("lo_ready")
        weights_used = sem("weights_used")
        const_in = sem("const_in")
        small_in = sem("small_in")
        x_in = [sem(f"x_in{i}") for i in range(4)]
        consts_done = sem("consts_done")
        x1_hi_ready = sem("x1_hi_ready")
        x1_ready = sem("x1_ready")
        sq_ready = sem("sq_ready")
        pool_step = sem("pool_step")
        win_step = sem("win_step")
        rope_step = sem("rope_step")
        rope_sin = sem("rope_sin")
        stat_sum, stat_var, stat_std, stat_inv = (sem(f"stat_{n}") for n in ("sum", "var", "std", "inv"))
        in_out = sem("in_out")
        lat_sq = sem("lat_sq")
        lat_norm = sem("lat_norm")
        lat_hi = sem("lat_hi")
        lat_ready = sem("lat_ready")
        key_turned = sem("key_turned")
        key_sum = sem("key_sum")
        key_ready = sem("key_ready")
        pooled = sem("pooled")
        pool_mixed = sem("pool_mixed")
        pool_hi = sem("pool_hi")
        x_again = sem("x_again")
        q_done, r_done = sem("q_done"), sem("r_done")
        act_proj = sem("act_proj")
        dve_proj = sem("dve_proj")
        v_made = sem("v_made")
        v_out = sem("v_out")
        v_copied = sem("v_copied")
        scores_done = sem("scores_done")
        neg_ready = sem("neg_ready")
        exp_ready = sem("exp_ready")
        sum_inv = sem("sum_inv")
        prob_ready = sem("prob_ready")
        turned = sem("turned")
        act_turned, dve_turned = sem("act_turned"), sem("dve_turned")
        mixed = sem("mixed")
        y_hi = sem("y_hi")
        y_ready = sem("y_ready")
        h_ready = sem("h_ready")
        x2_hi_ready = sem("x2_hi_ready")
        x2_ready = sem("x2_ready")
        h_sq = sem("h_sq")
        acc_step = sem("acc_step")
        keys_in = sem("keys_in")
        q_ready = sem("q_ready")
        s_done = sem("s_done")
        s_ready = sem("s_ready")
        topk_step = sem("topk_step")
        pick_ready = sem("pick_ready")
        picked_ready = sem("picked_ready")
        gate_in = sem("gate_in")
        gate_exp = sem("gate_exp")
        spill_out = sem("spill_out")
        spill_stored = sem("spill_stored")
        h_in = [sem(f"h_in{i}") for i in range(2)]
        hk_turned = sem("hk_turned")
        hk_ready = sem("hk_ready")
        oh_i = sem("oh_i")
        oh_g = sem("oh_g")
        oh_j = sem("oh_j")
        g_done = sem("g_done")
        g_out = sem("g_out")
        g_stored = [sem(f"g_stored{i}") for i in range(2)]
        g_in = [sem(f"g_in{i}") for i in range(2)]
        e_scaled, e_gelu, e_gated, e_hi, e_ready = (
            sem(f"e_{n}") for n in ("scaled", "gelu", "gated", "hi", "ready"))
        v_done = sem("v_done")
        v_added = sem("v_added")
        p_in = sem("p_in")
        p_hi, p_ready = sem("p_hi"), sem("p_ready")
        x3_hi_ready, x3_ready, h3_sq = (sem(f"x3_{n}") for n in ("hi", "ready", "sq"))
        proj_done, act_proj_out, dve_proj_out = sem("proj_done"), sem("act_proj_out"), sem("dve_proj_out")
        gate_pre, gate_sig, gate_mul, h_end = (sem(f"gate_{n}") for n in ("pre", "sig", "mul", "end"))
        end_sq = sem("end_sq")
        fin_ready = sem("fin_ready")
        out_stored = sem("out_stored")

        PER_TOPK = 20
        ROPE_STEPS = 11
        ACC = DC + 1

        def a_slot(m, par):
            return m if m or not par else GROUP

        def head_block(j):
            return j if j < HEAD_HALF else j - HEAD_HALF + 8

        def chunk(tensor, n):
            if isinstance(n, int):
                return tensor[:, n, :]
            return tensor[:, bass.ds(n, 1), :].rearrange("p a t -> p (a t)")

        def peer_unit(g, k):
            return g * PER_GROUP + U_PEER + 1 + k

        def peer_slot(k, par):
            return (U_PEER + 1 + k + par) % 2


        def spilled(n):
            return n * GROUP + GROUP - 1

        block = ctx.enter_context(nc.Block())

        @block.sync
        def _(sp):
            def load_unit(u, halves, parts=(0, 1)):
                for s in parts:
                    if not isinstance(u, int) or u > 0:
                        sp.wait_ge(lo_ready, 2 * u - 1 + s)
                    dst, src = halves(s)
                    sp.dma_start(dst, src).then_inc(raw_loaded[s], 16)

            def packed(w, n):
                return lambda s: (raw[s][:, :, :], w[n, :, 8 * s:8 * s + 8, :])

            def v_part(g, quarter):
                vr = v.rearrange("(g m e) (q c) -> g q e m c", g=N_GROUPS, m=GROUP, q=4)
                return lambda s: (raw[s][:, :, :].rearrange("p (m c) e -> p m (c e)", m=2),
                                  vr[g, quarter, :, 2 * s:2 * s + 2, :])

            sp.dma_start(gain[:, :], gains).then_inc(small_in, 16)
            for i in range(4):
                if i < 2:
                    load_unit(0, packed(w_in, 0), parts=(i,))
                sp.dma_start(h[:, 4 * i:4 * i + 4, :], x_t[:, 4 * i:4 * i + 4, :]).then_inc(x_in[i], 16)
            sp.dma_start(ident[:, :], consts[:, C_IDENT:C_IDENT + P]).then_inc(const_in, 16)
            sp.dma_start(iota[:, :], consts[:, C_IOTA:C_IOTA + P]).then_inc(const_in, 16)
            sp.dma_start(mask_f[:, :], consts[:, C_MASK:C_MASK + P]).then_inc(const_in, 16)
            sp.dma_start(dup[:, :], consts[:, C_DUP:C_DUP + P]).then_inc(const_in, 16)
            sp.dma_start(rope_c[:, :], rope_cols).then_inc(const_in, 16)
            sp.dma_start(p_inv[:, :, :], pool_inv).then_inc(const_in, 16)
            sp.dma_start(pool_wt[:, :, :], pool_w).then_inc(const_in, 16)
            sp.dma_start(pos_i[:, :], positions.to_broadcast([P, T])).then_inc(const_in, 16)
            with sp.Fori(1, N_IN) as n:
                load_unit(n, packed(w_in, n))

            def head_w(n):
                return lambda s: (raw[s][:, 0:HEAD_HALF, :], w_head[n, :, HEAD_HALF * s:HEAD_HALF * (s + 1), :])

            load_unit(U_HEAD0, head_w(0))
            for n in range(N_V):
                load_unit(U_V + n, packed(w_v, n))
            load_unit(U_HEAD + 1, head_w(1))
            sp.wait_ge(pool_mixed, 4)
            for i in range(4):
                sp.dma_start(h[:, 4 * i:4 * i + 4, :], x_t[:, 4 * i:4 * i + 4, :]).then_inc(x_again, 16)
            with sp.Fori(2, HEADS) as n:
                load_unit(n + U_HEAD, head_w(n))
            with sp.Fori(0, DC) as n:
                load_unit(n + U_WO, packed(w_o, n))
            load_unit(U_WQ, packed(w_q, 0))
            sp.wait_ge(weights_used, U_WQ)
            sp.dma_start(k_all[:, :, :], keys).then_inc(keys_in, 16)
            load_unit(U_WQ + 1, packed(w_q, 1))
            with sp.Fori(1, PH) as i:
                for k in range(2):
                    load_unit(4 * i + U_WQ - 2 + 2 * k, packed(w_q, 2 * i + k))
                    load_unit(4 * i + U_WQ - 1 + 2 * k, packed(u_t, spilled(2 * i - 2 + k)))
            for n in range(ALONE + 2):
                load_unit(U_ALONE + n, packed(u_t, spilled(2 * (PH - 1) + n)))

            def store_block(b, s):
                sp.wait_ge(g_out, (TB // OH) * 2 * (b + 1))
                sp.dma_start(g_dram[b], g_blk[s][:, :, :]).then_inc(g_stored[s], 16)

            with sp.Fori(0, N_TB // 2 - 2) as b2:
                for s in range(2):
                    load_unit(2 * b2 + s + U_BLOCK + 2, packed(u_t, spilled(2 * b2 + s + 2 * PH + 3)))
                    store_block(2 * b2 + s, s)
            load_unit(U_PEER - 1, packed(u_t, spilled(N_GROUPS - 1)))
            store_block(N_TB - 4, 0)
            for n in range(3):
                load_unit(U_PEER + n, packed(u_t, n))
                store_block(N_TB - 3 + n, (n + 1) % 2)
            for s in range(2):
                sp.wait_ge(g_stored[s], 16 * (N_TB // 2))
            sp.wait_ge(spill_stored, 16 * N_GROUPS)

            def load_g(g, par):
                sp.dma_start(g_tile[par][:, :, :, :],
                             g_dram[:, :, bass.ds(g * GROUP, GROUP), :].rearrange("b j i t -> j b i t")
                             ).then_inc(g_in[par], 16)
                sp.dma_start(h_pre[par][:, :], h_dram[g]).then_inc(h_in[par], 16)

            def peer_group(g, par, first=False, last=False):
                if not first:
                    for m in range(1, GROUP - 1):
                        load_unit(peer_unit(g, m - 1), packed(u_t, g * GROUP + m))
                if first:
                    load_unit(peer_unit(g, 2), packed(u_t, (g + 1) * GROUP))
                    load_g(g + 1, 1 - par)
                elif not last:
                    sp.wait_ge(e_gated, GROUP * g)
                    load_g(g + 1, 1 - par)
                    load_unit(peer_unit(g, 2), packed(u_t, (g + 1) * GROUP))
                for q in range(4):
                    load_unit(peer_unit(g, 3 + q - (1 if last else 0)), v_part(g, q))

            load_g(0, 0)
            peer_group(0, 0, first=True)
            sp.dma_start(pt[:, :, :], p_t).then_inc(p_in, 16)
            peer_group(1, 1)
            with sp.Fori(1, N_GROUPS // 2 - 1) as g2:
                peer_group(2 * g2, 0)
                peer_group(2 * g2 + 1, 1)
            peer_group(N_GROUPS - 2, 0)
            peer_group(N_GROUPS - 1, 1, last=True)
            for n in range(2):
                load_unit(U_PROJ + n, packed(w_proj, n))
            with sp.Fori(0, DC) as n:
                load_unit(n + U_GATE, packed(w_gate, n))
            for i in range(DC // 2):
                sp.wait_ge(fin_ready, 2 * i + 2)
                sp.dma_start(out_t[:, 2 * i:2 * i + 2, :], proj[:, 2 * i:2 * i + 2, :]).then_inc(out_stored, 16)
            sp.wait_ge(out_stored, 16 * (DC // 2))

        @block.tensor
        def _(pe):
            def passes(out, blk, slot, m_hi, m_lo, first, last):
                pe.matmul(out, w_hi[slot][:, blk, :], m_hi, start=first, stop=False)
                pe.matmul(out, w_hi[slot][:, blk, :], m_lo, start=False, stop=False)
                return pe.matmul(out, w_lo[slot][:, blk, :], m_hi, start=False, stop=last)

            def half_in(u, s):
                pe.wait_ge(lo_ready, 2 * u + 1 + s)

            def unit(u, slot, out, x_hi, x_lo, before=None, quarter_done=None):
                for b in range(16):
                    if b % 8 == 0:
                        half_in(u, b // 8)
                    if before:
                        before(b)
                    mm = passes(out[:, :], b, slot, x_hi[:, b, :], x_lo[:, b, :], b == 0, b == 15)
                    if b == 15:
                        mm.then_inc(weights_used, 1)
                    if quarter_done and b % 4 == 3:
                        quarter_done(b // 4)

            def in_unit(u, slot):
                if not isinstance(u, int) or u >= 2:
                    pe.wait_ge(in_out, u - 1)
                unit(u, slot, bank[slot], x1_hi, x1_lo)

            unit(0, 0, bank[0], x1_hi, x1_lo, before=lambda b: pe.wait_ge(x1_ready, b + 1))

            def x_sum(quarter):
                if quarter == 1:
                    pe.wait_ge(pool_step, DC - 1)
                    pe.matmul(bank[7][:, :], ones[:, :], x_acc[:, :], start=True, stop=True).then_inc(stat_sum, 1)

            unit(1, 1, bank[1], x1_hi, x1_lo, quarter_done=x_sum)
            with pe.Fori(1, 3) as i:
                in_unit(2 * i, 0)
                in_unit(2 * i + 1, 1)

            def latent_sum(i):
                pe.wait_ge(lat_sq, i + 1)
                pe.wait_ge(stat_var, i + 1)
                for c in range(LC):
                    mm = pe.matmul(bank[7][:, :], ones[:, :], sq_l[:, c, :], start=(c == 0), stop=(c == LC - 1))
                mm.then_inc(stat_sum, 1)

            latent_sum(0)
            with pe.Fori(0, 2) as i:
                in_unit(2 * i + 6, 0)
                in_unit(2 * i + 7, 1)
            latent_sum(1)
            pe.wait_ge(key_turned, 1)
            pe.matmul(bank[6][:, :], dup[:, :], key_p[:, :], start=True, stop=True).then_inc(key_sum, 1)
            in_unit(10, 0)
            in_unit(11, 1)
            in_unit(12, 0)

            def project(part, u, slot, out, lat):
                for c in range(LC):
                    blk = head_block(LC * part + c)
                    if blk % 8 == 0:
                        half_in(u, blk // 8)
                    mm = passes(out[:, :], blk, slot, l_hi[lat][:, c, :], l_lo[lat][:, c, :], c == 0, c == LC - 1)
                mm.then_inc((q_done, r_done, weights_used)[part], 1)

            def scores(hd):
                pe.wait_ge(act_proj, 2 * hd + 2)
                pe.wait_ge(dve_proj, hd + 1)
                for t in range(TC):
                    n = (t + 1) * P
                    ts = slice(t * P, n)
                    out = bank[2 + t]
                    pe.matmul(out[:, 0:n], q_n[:, ts], k_n[:, 0:n], start=True, stop=False)
                    pe.matmul(out[:, 0:n], q_r[:, ts], key_r[:, 0:n], start=False, stop=False)
                    pe.matmul(out[:, ts], ident_b[:, :], mask_b[:, :], start=False, stop=True)\
                      .then_inc(scores_done, 1)

            def turn_probs(hd, t):
                pe.wait_ge(prob_ready, 4 * hd + t + 1)
                if t == 0:
                    pe.wait_ge(y_ready, hd + 4)
                elif t >= 2:
                    pe.wait_ge(dve_turned if t == 2 else act_turned, 2 * hd + 1)
                out = bank[6 + t % 2]
                for c in range(t + 1):
                    mm = pe.transpose(out[:, c * P:(c + 1) * P], prob[:, t * (t + 1) // 2 + c, :], ident[:, :])
                mm.then_inc(turned, 1)

            def mix_head(hd, par):
                pe.wait_ge(dve_turned, 2 * hd + 2)
                pe.wait_ge(act_turned, 2 * hd + 2)
                pe.wait_ge(v_copied, hd + 1)
                for c in range(TC):
                    mm = pe.matmul(bank[6][:, c * P:T], v_h[par][:, c, :], prob_t[:, c, c * P:T],
                                   start=(c == 0), stop=(c == TC - 1))
                mm.then_inc(mixed, 1)

            def head(hd, slot, par):
                u = hd + U_HEAD
                pe.wait_ge(act_proj, 2 * hd)
                project(0, u, slot, bank[0], 0)
                pe.wait_ge(dve_proj, hd)
                project(1, u, slot, bank[1], 0)
                turn_probs(hd - 1, 0)
                turn_probs(hd - 1, 1)
                pe.wait_ge(act_proj, 2 * hd + 1)
                project(2, u, slot, bank[0], 1)
                turn_probs(hd - 1, 2)
                turn_probs(hd - 1, 3)
                scores(hd)
                mix_head(hd - 1, par)

            pe.wait_ge(lat_ready, 2 * LC)
            pe.wait_ge(in_out, N_IN)
            project(0, U_HEAD0, U_HEAD0 % 2, bank[0], 0)
            project(1, U_HEAD0, U_HEAD0 % 2, bank[1], 0)
            pe.wait_ge(act_proj, 1)
            project(2, U_HEAD0, U_HEAD0 % 2, bank[0], 1)
            pe.wait_ge(key_ready, 1)
            def values(n):
                slot = (U_V + n) % 2
                for t in range(TC):
                    ts = slice(t * P, (t + 1) * P)
                    if n == N_V - 1 and t < 2:
                        pe.wait_ge(y_ready, 3 + t)
                    elif 4 * n + t >= 2:
                        pe.wait_ge(v_out, 4 * n + t - 1)
                    out = bank[6 + t % 2][:, :]
                    for c in range(LC):
                        if t == 0 and c % 2 == 0:
                            half_in(U_V + n, c // 2)
                        hi_c = w_hi[slot][:, 4 * c:4 * c + 4, :].rearrange("p h d -> p (h d)")
                        lo_c = w_lo[slot][:, 4 * c:4 * c + 4, :].rearrange("p h d -> p (h d)")
                        pe.matmul(out, l_hi[1][:, c, ts], hi_c, start=(c == 0), stop=False)
                        pe.matmul(out, l_hi[1][:, c, ts], lo_c, start=False, stop=False)
                        mm = pe.matmul(out, l_lo[1][:, c, ts], hi_c, start=False, stop=(c == LC - 1))
                    mm.then_inc(v_made if t < TC - 1 else weights_used, 1)

            for n in range(N_V - 1):
                values(n)
            for g in range(4):
                pe.wait_ge(pooled, g + 1)
                if g < 2:
                    pe.wait_ge(v_out, 4 * (N_V - 1) - 1 + g)
                else:
                    pe.wait_ge(y_ready, g - 1)
                pe.matmul(bank[6 + g % 2][:, :], pool_wt[:, g, :], z[:, 9 + g, :], start=True, stop=True)\
                  .then_inc(pool_mixed, 1)
            values(N_V - 1)
            scores(0)
            with pe.Fori(0, (HEADS - 2) // 2) as i:
                for k in range(2):
                    head(2 * i + 1 + k, (U_HEAD + 1 + k) % 2, k)
            head(HEADS - 1, (U_HEAD + HEADS - 1) % 2, 0)

            def last_head(b):
                if b == 8:
                    for t in range(TC):
                        turn_probs(HEADS - 1, t)
                if b == 13:
                    mix_head(HEADS - 1, 1)
                pe.wait_ge(y_ready, b + 1)

            pe.wait_ge(act_proj, 2 * HEADS)
            pe.wait_ge(dve_proj, HEADS)
            unit(U_WO, U_WO % 2, bank[0], x1_hi, x1_lo, before=last_head)
            unit(U_WO + 1, (U_WO + 1) % 2, bank[1], x1_hi, x1_lo)
            with pe.Fori(1, DC // 2) as i:
                for k in range(2):
                    pe.wait_ge(h_ready, 2 * i + k - 1)
                    unit(2 * i + k + U_WO, (U_WO + k) % 2, bank[k], x1_hi, x1_lo)

            def key_scores(n, k):
                pe.wait_ge(q_ready, n + 1)
                for t in range(TC):
                    mm = pe.matmul(bank[2 + k][:, t * P:(t + 1) * P], q_f[k][:, t * P:(t + 1) * P],
                                   chunk(k_all, n), start=True, stop=True)
                mm.then_inc(s_done, 1)

            pe.wait_ge(x2_ready, DC)
            unit(U_WQ, U_WQ % 2, bank[0], x2_hi, x2_lo)
            pe.wait_ge(acc_step, ACC)
            pe.matmul(bank[7][:, :], ones[:, :], acc[:, :], start=True, stop=True).then_inc(stat_sum, 1)
            unit(U_WQ + 1, (U_WQ + 1) % 2, bank[1], x2_hi, x2_lo)
            pe.wait_ge(keys_in, 16)
            key_scores(0, 0)

            def spill(n, k, u, slot, quarter_done=None):
                if not isinstance(n, int) or n >= 2:
                    pe.wait_ge(spill_out, n - 1)
                unit(u, slot, bank[4 + k], x2_hi, x2_lo, quarter_done=quarter_done)

            def query_head(hd):
                for k in range(2):
                    n = 2 * hd + k
                    pe.wait_ge(q_ready, n - 1)
                    unit(4 * hd + U_WQ - 2 + 2 * k, U_WQ % 2, bank[k], x2_hi, x2_lo)
                    if not isinstance(n, int) or n > 2:
                        pe.wait_ge(s_ready, n - 2)
                    key_scores(n - 1, (k + 1) % 2)
                    spill(n - 2, k, 4 * hd + U_WQ - 1 + 2 * k, (U_WQ + 1) % 2)

            query_head(1)
            with pe.Fori(2, PH) as hd:
                query_head(hd)
            pe.wait_ge(s_ready, 2 * PH - 2)
            key_scores(2 * PH - 1, 1)
            for e in range(ALONE):
                spill(2 * (PH - 1) + e, e % 2, U_ALONE + e, (U_ALONE + e) % 2)

            pe.wait_ge(topk_step, PER_TOPK * PH)
            pe.wait_ge(s_ready, 2 * PH)
            for i in range(3):
                for t in range(TC):
                    mm = pe.transpose(bank[i][:, t * P:(t + 1) * P],
                                      sel[i][:, t, :, :].rearrange("p h k -> p (h k)"), ident[:, :])
                mm.then_inc(hk_turned, 1)

            def g_group(q, s, first=False):
                pe.wait_ge(oh_g, q + 1)
                pe.wait_ge(oh_j, q + 1)
                for half in range(2):
                    out = bank[6 + half]
                    if not first:
                        pe.wait_ge(g_out, 2 * q - 1 + half)
                    for t in range(4):
                        o = 4 * half + t
                        mm = pe.matmul(out[:, t * P:(t + 1) * P], one_j[s][:, o, :], one_g[s][:, o, :],
                                       start=True, stop=True)
                    mm.then_inc(g_done, 1)

            def g_block(b, k):
                n = b + 2 * (PH - 1) + ALONE
                spill(n, (ALONE + k) % 2, b + U_BLOCK, (U_BLOCK + k) % 2, quarter_done=groups(b))

            def groups(b):
                return lambda e: g_group(b * (TB // OH) + e, e % 2, first=isinstance(b, int) and b == 0 and e == 0)

            g_block(0, 0)
            g_block(1, 1)
            with pe.Fori(1, N_TB // 2 - 1) as b2:
                for k in range(2):
                    g_block(2 * b2 + k, k)
            g_block(N_TB - 2, 0)
            unit(U_PEER, U_PEER % 2, bank[0], x2_hi, x2_lo, quarter_done=groups(N_TB - 1))

            def first_product(u, slot, b, scaled):
                if scaled is not None:
                    pe.wait_ge(e_scaled, scaled)
                unit(u, slot, bank[b], x2_hi, x2_lo)

            def second_product(g, par, q, u, slot, first=False):
                if q == 0:
                    pe.wait_ge(e_ready, GROUP * g + GROUP)
                half_in(u, 0)
                half_in(u, 1)
                for c in range(4):
                    if not (first and q == 0):
                        pe.wait_ge(v_added, 16 * g + 4 * q - 3 + c)
                    for m in range(GROUP):
                        a = a_slot(m, par)
                        mm = passes(bank[2 + c][:, :], 4 * m + c, slot, a_hi[a][:, :], a_lo[a][:, :],
                                    m == 0, m == GROUP - 1)
                    mm.then_inc(v_done if c < 3 else weights_used, 1)

            def peer_group(g, par, first=False, last=False):
                for k, scaled in enumerate((g * GROUP, g * GROUP + 1, g * GROUP + 2)[:2 if last else 3]):
                    first_product(peer_unit(g, k), peer_slot(k, par), (1 + k + par) % 2,
                                  scaled=None if first and k == 0 else scaled)
                for q in range(4):
                    k = 3 + q - (1 if last else 0)
                    second_product(g, par, q, peer_unit(g, k), peer_slot(k, par), first)

            peer_group(0, 0, first=True)
            peer_group(1, 1)
            with pe.Fori(1, N_GROUPS // 2 - 1) as g2:
                peer_group(2 * g2, 0)
                peer_group(2 * g2 + 1, 1)
            peer_group(N_GROUPS - 2, 0)
            peer_group(N_GROUPS - 1, 1, last=True)

            pe.wait_ge(p_ready, 2)
            for n in range(DC):
                u, b = U_PROJ + n // 8, n % 8 * 2
                if n % 4 == 0:
                    half_in(u, n // 4 % 2)
                if n >= 4:
                    pe.wait_ge(dve_proj_out if n % 2 else act_proj_out, n // 2 - 1)
                elif n >= 2:
                    pe.wait_ge(v_added, 16 * N_GROUPS - 5 + n)
                for c in range(2):
                    mm = passes(bank[n % 4][:, :], b + c, u % 2, pt_hi[:, c, :], pt_lo[:, c, :], c == 0, c == 1)
                mm.then_inc(weights_used if n % 8 == 7 else proj_done, 1)
            pe.wait_ge(x3_ready, DC)
            pe.wait_ge(act_proj_out, DC // 2)
            pe.wait_ge(dve_proj_out, DC // 2)
            unit(U_GATE, U_GATE % 2, bank[0], x2_hi, x2_lo)
            pe.wait_ge(acc_step, 2 * ACC)
            pe.matmul(bank[7][:, :], ones[:, :], acc[:, :], start=True, stop=True).then_inc(stat_sum, 1)
            unit(U_GATE + 1, (U_GATE + 1) % 2, bank[1], x2_hi, x2_lo)
            with pe.Fori(1, DC // 2) as i:
                for k in range(2):
                    pe.wait_ge(gate_pre, 2 * i + k - 1)
                    unit(2 * i + k + U_GATE, (U_GATE + k) % 2, bank[k], x2_hi, x2_lo)
            pe.wait_ge(acc_step, 3 * ACC)
            pe.matmul(bank[7][:, :], ones[:, :], acc[:, :], start=True, stop=True).then_inc(stat_sum, 1)

        @block.scalar
        def _(act):
            def hi(u, slot, halves=(0, 1), n=8):
                for s in halves:
                    act.wait_ge(raw_loaded[s], 16 * u + 16)
                    if s == 0 and not (isinstance(u, int) and u < 2):
                        act.wait_ge(weights_used, u - 1)
                    act.activation(w_hi[slot][:, 8 * s:8 * s + n, :], raw[s][:, 0:n, :], ACT.Copy)\
                       .then_inc(hi_ready, 1)

            def alone():
                act.wait_ge(small_in, 16)

            def std(k, buf):
                act.wait_ge(stat_var, k + 1)
                act.activation(buf[:, :], buf[:, :], ACT.Sqrt).then_inc(stat_std, 1)

            act.wait_ge(small_in, 16)
            for i in range(4):
                if i < 2:
                    hi(0, 0, halves=(i,))
                act.wait_ge(x_in[i], 16)
                for c in range(4 * i, 4 * i + 4):
                    act.activation(x1_hi[:, c, :], h[:, c, :], ACT.Copy, scale=gain[:, c:c + 1])\
                       .then_inc(x1_hi_ready, 1)
                if i == 3:
                    hi(1, 1)
                for c in range(4 * i, 4 * i + 4):
                    act.activation(sq_x[:, c, :], h[:, c, :], ACT.Square).then_inc(sq_ready, 1)
            act.wait_ge(rope_step, ROPE_STEPS)
            act.activation(table[:, :], ang[:, :], ACT.Sin).then_inc(rope_sin, 1)
            std(0, rinv)
            with act.Fori(0, 2) as i:
                hi(2 * i + 2, 0)
                hi(2 * i + 3, 1)

            def latent_sq(i):
                act.wait_ge(in_out, 4 * i + 4)
                act.activation(sq_l[:, :, :], z[:, 4 * i:4 * i + 4, :], ACT.Square).then_inc(lat_sq, 1)

            def latent_hi(i):
                for c in range(LC):
                    act.wait_ge(lat_norm, 4 * i + c + 1)
                    act.activation(l_hi[i][:, c, :], z[:, 4 * i + c, :], ACT.Copy).then_inc(lat_hi, 1)

            hi(6, 0)
            latent_sq(0)
            std(1, rinv_l)
            latent_hi(0)
            with act.Fori(0, 2) as i:
                hi(2 * i + 7, 1)
                hi(2 * i + 8, 0)
            latent_sq(1)
            hi(11, 1)
            std(2, rinv_l)
            latent_hi(1)
            hi(12, 0)
            act.wait_ge(key_sum, 1)
            act.activation(key_r[:, :], bank[6][:, :], ACT.Copy).then_inc(key_ready, 1)
            hi(U_HEAD0, U_HEAD0 % 2, n=HEAD_HALF)

            def head_q(hd):
                act.wait_ge(q_done, hd + 1)
                act.activation(q_n[:, :], bank[0][:, :], ACT.Copy, scale=SCALE).then_inc(act_proj, 1)

            def head_k(u):
                act.wait_ge(weights_used, u + 1)
                act.activation(k_n[:, :], bank[0][:, :], ACT.Copy).then_inc(act_proj, 1)

            def head_turned(hd, t):
                act.wait_ge(turned, 4 * hd + t + 1)
                act.activation(prob_t[:, 0:t + 1, t * P:(t + 1) * P],
                               bank[7][:, 0:(t + 1) * P].rearrange("p (c q) -> p c q", q=P), ACT.Copy)\
                   .then_inc(act_turned, 1)

            def head_mixed(hd, y):
                alone()
                act.wait_ge(mixed, hd + 1)
                act.activation(y, bank[6][:, :], ACT.Copy).then_inc(y_hi, 1)

            def head_exp(hd):
                for t in range(TC):
                    lo, n = t * (t + 1) // 2, t + 1
                    act.wait_ge(neg_ready, 4 * hd + t + 1)
                    act.activation(prob[:, lo:lo + n, :].rearrange("p c k -> p (c k)"), bank[2 + t][:, 0:n * P],
                                   ACT.Exp, bias=neg_max[:, t:t + 1], accum_out=row_sum[:, t:t + 1])\
                       .then_inc(exp_ready, 1)

            def head(hd, slot, n=HEAD_HALF):
                u = hd + U_HEAD
                hi(u + 1, 1 - slot, n=n)
                head_q(hd)
                head_turned(hd - 1, 1)
                head_k(u)
                head_turned(hd - 1, 3)
                head_exp(hd)
                head_mixed(hd - 1, chunk(x1_hi, hd + 3))

            hi(U_V, U_V % 2)
            head_q(0)
            head_k(U_HEAD0)
            for n in range(1, N_V):
                hi(U_V + n, (U_V + n) % 2)
            for g in range(4):
                act.wait_ge(pool_mixed, g + 1)
                act.activation(x1_hi[:, g, :], bank[6 + g % 2][:, :], ACT.Copy,
                               scale=gain[:, G_POOL - C_GAIN + g:G_POOL - C_GAIN + g + 1]).then_inc(pool_hi, 1)
            hi(U_HEAD + 1, (U_HEAD + 1) % 2, n=HEAD_HALF)
            head_exp(0)
            with act.Fori(0, (HEADS - 2) // 2) as i:
                for k in range(2):
                    head(2 * i + 1 + k, (U_HEAD + 1 + k) % 2)
            head(HEADS - 1, (U_HEAD + HEADS - 1) % 2, n=8)
            head_turned(HEADS - 1, 1)
            head_turned(HEADS - 1, 3)
            head_mixed(HEADS - 1, x1_hi[:, HEADS + 3, :])

            def residual_out(n, k):
                hi(n + U_WO + 1, (U_WO + 1 + k) % 2)
                alone()
                act.wait_ge(h_ready, n + 1)
                act.activation(chunk(x2_hi, n), chunk(h, n), ACT.Copy, scale=gain[:, bass.ds(n + G_FFN - C_GAIN, 1)])\
                   .then_inc(x2_hi_ready, 1)
                if not isinstance(n, int):
                    alone()
                    act.wait_ge(acc_step, n)
                act.activation(bank[2 + k][:, :], chunk(h, n), ACT.Square).then_inc(h_sq, 1)

            residual_out(0, 0)
            residual_out(1, 1)
            with act.Fori(1, DC // 2) as i:
                for k in range(2):
                    residual_out(2 * i + k, k)

            def score_out(n, k):
                act.wait_ge(s_done, n + 1)
                act.activation(s_f[k][:, :, :].rearrange("p t n -> p (t n)"), bank[2 + k][:, :], ACT.Copy)\
                   .then_inc(s_ready, 1)

            def gates(hd):
                act.wait_ge(gate_in, hd + 1)
                act.activation(b_exp[:, :, :], b_exp[:, :, :], ACT.Exp).then_inc(gate_exp, 1)

            def spill(n, k, u):
                if not isinstance(n, int) or n >= 1:
                    alone()
                    act.wait_ge(spill_stored, 16 * n)
                act.wait_ge(weights_used, u + 1)
                act.activation(h_out[:, :], bank[4 + k][:, :], ACT.Copy).then_inc(spill_out, 1)
                act.wait_ge(spill_out, n + 1)
                act.dma_start(h_dram[n], h_out[:, :]).then_inc(spill_stored, 16)

            hi(U_WQ + 1, (U_WQ + 1) % 2)
            std(3, rinv)
            hi(U_WQ + 2, U_WQ % 2)
            score_out(0, 0)

            def choice(i):
                u = 4 * i + U_WQ - 2
                hi(u + 1, (U_WQ + 1) % 2)
                score_out(2 * i - 1, 1)
                hi(u + 2, U_WQ % 2)
                spill(2 * i - 2, 0, u + 1)
                hi(u + 3, (U_WQ + 1) % 2)
                score_out(2 * i, 0)
                hi(u + 4, U_WQ % 2)
                gates(i - 1)
                spill(2 * i - 1, 1, u + 3)

            choice(1)
            with act.Fori(2, PH) as i:
                choice(i)
            score_out(2 * PH - 1, 1)
            for e in range(ALONE):
                hi(U_ALONE + e + 1, (U_ALONE + e + 1) % 2)
                if e == ALONE - 1:
                    gates(PH - 1)
                spill(2 * (PH - 1) + e, e % 2, U_ALONE + e)

            for i in range(3):
                act.wait_ge(hk_turned, i + 1)
                act.activation(hk_t[i][:, :], bank[i][:, :], ACT.Copy).then_inc(hk_ready, 1)

            def g_evict(b, s, q):
                for half in range(2):
                    act.wait_ge(g_done, 2 * ((TB // OH) * b + q) + half + 1)
                    t0 = OH * q + 4 * half
                    act.activation(g_blk[s][:, :, t0:t0 + 4].rearrange("p i t -> p t i"),
                                   bank[6 + half][:, :].rearrange("p (t i) -> p t i", i=NK), ACT.Copy)\
                       .then_inc(g_out, 1)

            def g_block(b, s, last=False):
                g_evict(b, s, 0)
                hi(b + U_BLOCK + 1, (U_BLOCK + 1 + s) % 2, halves=(0,))
                g_evict(b, s, 1)
                hi(b + U_BLOCK + 1, (U_BLOCK + 1 + s) % 2, halves=(1,))
                g_evict(b, s, 2)
                if not last:
                    spill(b + 2 * (PH - 1) + ALONE, (ALONE + s) % 2, b + U_BLOCK)
                g_evict(b, s, 3)

            for s in range(2):
                g_block(s, s)
            with act.Fori(1, N_TB // 2 - 1) as b2:
                for s in range(2):
                    act.wait_ge(g_stored[s], 16 * b2)
                    g_block(2 * b2 + s, s)
            for s in range(2):
                act.wait_ge(g_stored[s], 16 * (N_TB // 2 - 1))
                g_block(N_TB - 2 + s, s, last=s == 1)

            def gelu(j):
                act.wait_ge(e_scaled, j + 1)
                act.activation(h_g[:, :], h_s[:, :], ACT.Gelu_apprx_tanh).then_inc(e_gelu, 1)

            def gated_hi(j, a):
                act.wait_ge(e_gated, j + 1)
                act.activation(a_hi[a][:, :], h_a[:, :], ACT.Copy).then_inc(e_hi, 1)

            def activate(j, a):
                gelu(j)
                gated_hi(j, a)

            def third_hi(c):
                act.wait_ge(v_added, 16 * (N_GROUPS - 1) + c + 1)
                act.activation(x2_hi[:, c, :], h[:, c, :], ACT.Copy,
                               scale=gain[:, G_PLE - C_GAIN + c:G_PLE - C_GAIN + c + 1]).then_inc(x3_hi_ready, 1)
                if c >= 2:
                    act.wait_ge(acc_step, ACC + c)
                act.activation(sq_h[c % 2][:, :], h[:, c, :], ACT.Square).then_inc(h3_sq, 1)

            def peer_group(g, par, first=False, last=False):
                p = g * GROUP + 1
                if first:
                    hi(peer_unit(g, 1), peer_slot(1, par))
                    gelu(0)
                    hi(peer_unit(g, 2), peer_slot(2, par))
                    gated_hi(0, a_slot(0, par))
                    activate(p, a_slot(1, par))
                else:
                    hi(peer_unit(g, 1), peer_slot(1, par))
                    activate(p, a_slot(1, par))
                    hi(peer_unit(g, 2), peer_slot(2, par))
                activate(p + 1, a_slot(3, par))
                activate(p + 2, a_slot(2, par))
                if not last:
                    hi(peer_unit(g, 3), peer_slot(3, par))
                    activate(p + 3, a_slot(0, 1 - par))
                for q in range(4):
                    k = 4 + q - (1 if last else 0)
                    hi(peer_unit(g, k), peer_slot(k, par))
                    if last:
                        for c in range(4 * q, 4 * q + 4):
                            third_hi(c)

            for s in range(2):
                act.wait_ge(g_stored[s], 16 * (N_TB // 2))
            peer_group(0, 0, first=True)
            act.wait_ge(p_in, 16)
            for c in range(2):
                act.activation(pt_hi[:, c, :], pt[:, c, :], ACT.Copy).then_inc(p_hi, 1)
            peer_group(1, 1)
            with act.Fori(1, N_GROUPS // 2 - 1) as g2:
                peer_group(2 * g2, 0)
                peer_group(2 * g2 + 1, 1)
            peer_group(N_GROUPS - 2, 0)
            peer_group(N_GROUPS - 1, 1, last=True)

            hi(U_PROJ + 1, (U_PROJ + 1) % 2)
            for n in range(0, DC, 2):
                if n == 8:
                    hi(U_GATE, U_GATE % 2)
                act.wait_ge(proj_done, n + 1 - n // 8)
                act.activation(proj[:, n, :], bank[n % 4][:, :], ACT.Copy).then_inc(act_proj_out, 1)
            hi(U_GATE + 1, (U_GATE + 1) % 2)
            std(4, rinv)

            def gate_out(n, k, more=True):
                if more:
                    hi(n + U_GATE + 1, (U_GATE + 1 + k) % 2)
                act.wait_ge(gate_pre, n + 1)
                act.activation(g_sig[:, :], g_pre[:, :], ACT.Sigmoid).then_inc(gate_sig, 1)
                alone()
                act.wait_ge(h_end, n + 1)
                act.activation(bank[2 + k][:, :], chunk(h, n), ACT.Square).then_inc(end_sq, 1)

            act.wait_ge(gate_pre, 1)
            act.activation(g_sig[:, :], g_pre[:, :], ACT.Sigmoid).then_inc(gate_sig, 1)
            act.wait_ge(h_end, 1)
            act.activation(bank[2][:, :], h[:, 0, :], ACT.Square).then_inc(end_sq, 1)
            with act.Fori(0, (DC - 2) // 2) as i:
                gate_out(2 * i + 1, 1)
                gate_out(2 * i + 2, 0)
            gate_out(DC - 1, 1, more=False)
            std(5, rinv)

        @block.vector
        def _(dve):
            def lo(u, slot, halves=(0, 1), n=8):
                for s in halves:
                    dve.wait_ge(hi_ready, 2 * u + s + 1)
                    dve.tensor_tensor(w_lo[slot][:, 8 * s:8 * s + n, :], raw[s][:, 0:n, :],
                                      w_hi[slot][:, 8 * s:8 * s + n, :].bitcast(F32), ALU.subtract)\
                       .then_inc(lo_ready, 1)

            def inverse(k, buf, n):
                dve.wait_ge(stat_sum, k + 1)
                dve.tensor_scalar(buf[:, :], bank[7][:, :], 1.0 / n, EPS, ALU.mult, ALU.add).then_inc(stat_var, 1)
                dve.wait_ge(stat_std, k + 1)
                dve.reciprocal(buf[:, :], buf[:, :]).then_inc(stat_inv, 1)
                dve.wait_ge(stat_inv, k + 1)

            dve.memset(ones[:, :], 1.0).then_inc(consts_done, 1)
            for c in range(DC):
                if c % 4 == 0 and c < 8:
                    lo(0, 0, halves=(c // 4,))
                dve.wait_ge(x1_hi_ready, c + 1)
                dve.scalar_tensor_tensor(x1_lo[:, c, :], h[:, c, :], gain[:, c:c + 1],
                                         x1_hi[:, c, :].bitcast(F32), ALU.mult, ALU.subtract).then_inc(x1_ready, 1)
            lo(1, 1)
            dve.wait_ge(const_in, 16 * 8)
            dve.tensor_copy(ident_b[:, :], ident[:, :]).then_inc(consts_done, 1)
            dve.tensor_copy(mask_b[:, :], mask_f[:, :]).then_inc(consts_done, 1)
            rope = [0]

            def rope_do(ins):
                rope[0] += 1
                ins.then_inc(rope_step, 1)
                dve.wait_ge(rope_step, rope[0])

            two_pi = 2 * np.pi
            c1 = 6.28125
            c2 = float(np.float32(round((two_pi - c1) * 2 ** 21) / 2 ** 21))
            c3 = float(np.float32(two_pi - c1 - c2))
            magic = 1.5 * 2 ** 23
            rope_do(dve.tensor_copy(ang[:, :], pos_i[:, :]))
            rope_do(dve.tensor_scalar(ang[:, :], ang[:, :], rope_c[:, 0:1], None, ALU.mult))
            rope_do(dve.tensor_scalar(turn[:, :], ang[:, :], 1 / two_pi, magic, ALU.mult, ALU.add))
            rope_do(dve.tensor_scalar(turn[:, :], turn[:, :], -magic, None, ALU.add))
            for c in (c1, c2, c3):
                rope_do(dve.scalar_tensor_tensor(ang[:, :], turn[:, :], -c, ang[:, :], ALU.mult, ALU.add))
            rope_do(dve.tensor_scalar(ang[:, :], ang[:, :], rope_c[:, 1:2], None, ALU.add))
            rope_do(dve.tensor_scalar(turn[:, :], ang[:, :], float(np.float32(np.pi)), -two_pi, ALU.is_gt, ALU.mult))
            rope_do(dve.tensor_tensor(ang[:, :], ang[:, :], turn[:, :], ALU.add))
            rope_do(dve.tensor_scalar(ang[:, :], ang[:, :], 3.1415925, -3.1415925, ALU.min, ALU.max))
            assert rope[0] == ROPE_STEPS

            inverse(0, rinv, D)

            def in_evict(u, slot):
                dve.wait_ge(weights_used, u + 1)
                dve.tensor_tensor(chunk(z, u), bank[slot][:, :], rinv[:, :], ALU.mult).then_inc(in_out, 1)

            def latent(i):
                inverse(i + 1, rinv_l, LC * P)
                for c in range(LC):
                    zc = z[:, 4 * i + c, :]
                    dve.scalar_tensor_tensor(zc, zc, gain[:, G_Q - C_GAIN + 4 * i + c:G_Q - C_GAIN + 4 * i + c + 1],
                                             rinv_l[:, :], ALU.mult, ALU.mult).then_inc(lat_norm, 1)
                for c in range(LC):
                    dve.wait_ge(lat_hi, 4 * i + c + 1)
                    dve.tensor_tensor(l_lo[i][:, c, :], z[:, 4 * i + c, :], l_hi[i][:, c, :].bitcast(F32),
                                      ALU.subtract).then_inc(lat_ready, 1)

            in_evict(0, 0)
            with dve.Fori(0, 2) as i:
                lo(2 * i + 2, 0)
                in_evict(2 * i + 1, 1)
                lo(2 * i + 3, 1)
                in_evict(2 * i + 2, 0)
            lo(6, 0)
            in_evict(5, 1)
            latent(0)
            with dve.Fori(0, 2) as i:
                lo(2 * i + 7, 1)
                in_evict(2 * i + 6, 0)
                lo(2 * i + 8, 0)
                in_evict(2 * i + 7, 1)
            dve.wait_ge(in_out, 9)
            dve.wait_ge(rope_sin, 1)
            dve.tensor_tensor(key_p[:, :], z[:, 8, :], table[:, :], ALU.mult).then_inc(key_turned, 1)
            lo(11, 1)
            latent(1)
            in_evict(10, 0)
            lo(12, 0)
            in_evict(11, 1)
            lo(U_HEAD0, U_HEAD0 % 2, n=HEAD_HALF)
            in_evict(12, 0)

            def head_rv(hd):
                dve.wait_ge(r_done, hd + 1)
                dve.scalar_tensor_tensor(q_r[:, :], bank[1][:, :], SCALE, table[:, :], ALU.mult, ALU.mult)\
                   .then_inc(dve_proj, 1)

            def values_out(n):
                for t in range(TC):
                    if t < TC - 1:
                        dve.wait_ge(v_made, (TC - 1) * n + t + 1)
                    else:
                        dve.wait_ge(weights_used, U_V + n + 1)
                    dve.tensor_copy(v_all[:, 4 + 4 * n:8 + 4 * n, t * P:(t + 1) * P],
                                    bank[6 + t % 2][:, :].rearrange("p (h d) -> p h d", h=4)).then_inc(v_out, 1)

            def head_turned(hd, t):
                dve.wait_ge(turned, 4 * hd + t + 1)
                dve.tensor_copy(prob_t[:, 0:t + 1, t * P:(t + 1) * P],
                                bank[6][:, 0:(t + 1) * P].rearrange("p (c q) -> p c q", q=P)).then_inc(dve_turned, 1)

            def head_mixed(hd, n):
                dve.wait_ge(y_hi, hd + 1)
                dve.tensor_tensor(chunk(x1_lo, n), bank[6][:, :], chunk(x1_hi, n).bitcast(F32), ALU.subtract)\
                   .then_inc(y_ready, 1)

            def head_softmax(hd):
                for t in range(TC):
                    dve.wait_ge(scores_done, 4 * hd + t + 1)
                    dve.tensor_reduce(neg_max[:, t:t + 1], bank[2 + t][:, 0:(t + 1) * P], AX.X, ALU.max, negate=True)\
                       .then_inc(neg_ready, 1)
                dve.wait_ge(exp_ready, 4 * hd + 4)
                dve.reciprocal(row_inv[:, :], row_sum[:, :]).then_inc(sum_inv, 1)
                dve.wait_ge(sum_inv, hd + 1)
                for t in range(TC):
                    a = t * (t + 1) // 2
                    pt_ = prob[:, a:a + t + 1, :]
                    dve.tensor_scalar(pt_, pt_, row_inv[:, t:t + 1], None, ALU.mult).then_inc(prob_ready, 1)

            lo(U_V, U_V % 2)
            head_rv(0)
            for n in range(N_V - 1):
                lo(U_V + n + 1, (U_V + n + 1) % 2)
                values_out(n)
            for g in range(4):
                dve.wait_ge(pool_hi, g + 1)
                dve.scalar_tensor_tensor(x1_lo[:, g, :], bank[6 + g % 2][:, :],
                                         gain[:, G_POOL - C_GAIN + g:G_POOL - C_GAIN + g + 1],
                                         x1_hi[:, g, :].bitcast(F32), ALU.mult, ALU.subtract).then_inc(y_ready, 1)
            lo(U_HEAD + 1, (U_HEAD + 1) % 2, n=HEAD_HALF)
            values_out(N_V - 1)
            head_softmax(0)

            def head(hd, slot, n=HEAD_HALF):
                lo(hd + U_HEAD + 1, 1 - slot, n=n)
                head_rv(hd)
                head_turned(hd - 1, 0)
                head_turned(hd - 1, 2)
                head_softmax(hd)
                head_mixed(hd - 1, hd + 3)

            with dve.Fori(0, (HEADS - 2) // 2) as i:
                for k in range(2):
                    head(2 * i + 1 + k, (U_HEAD + 1 + k) % 2)
            head(HEADS - 1, (U_HEAD + HEADS - 1) % 2, n=8)
            head_turned(HEADS - 1, 0)
            head_turned(HEADS - 1, 2)
            head_mixed(HEADS - 1, HEADS + 3)

            def acc_clear():
                dve.memset(acc[:, :], 0.0).then_inc(acc_step, 1)

            def acc_add(a, n, b, squares):
                dve.wait_ge(squares, n + 1)
                dve.wait_ge(acc_step, ACC * a + n + 1)
                dve.tensor_tensor(acc[:, :], acc[:, :], bank[b][:, :], ALU.add).then_inc(acc_step, 1)

            acc_clear()
            dve.wait_ge(x_again, 64)
            with dve.Fori(0, DC // 2) as i:
                for k in range(2):
                    n = 2 * i + k
                    lo(n + U_WO + 1, (U_WO + 1 + k) % 2)
                    dve.wait_ge(weights_used, n + U_WO + 1)
                    dve.tensor_tensor(chunk(h, n), bank[k][:, :], chunk(h, n), ALU.add).then_inc(h_ready, 1)
                    dve.wait_ge(x2_hi_ready, n + 1)
                    dve.scalar_tensor_tensor(chunk(x2_lo, n), chunk(h, n), gain[:, bass.ds(n + G_FFN - C_GAIN, 1)],
                                             chunk(x2_hi, n).bitcast(F32), ALU.mult, ALU.subtract)\
                       .then_inc(x2_ready, 1)
                    acc_add(0, n, 2 + k, h_sq)

            def before_max(semaphore, value):
                dve.wait_ge(semaphore, value)
                dve.tensor_copy(carrier[:, :], iota[:, 0:1])

            def step_by_step(done):
                k = [0]

                def step(ins, max_next=False):
                    k[0] += 1
                    ins.then_inc(topk_step, 1)
                    if max_next:
                        before_max(topk_step, done + k[0])
                    else:
                        dve.wait_ge(topk_step, done + k[0])
                return step, k

            def query_out(n, k, u):
                dve.wait_ge(weights_used, u + 1)
                dve.tensor_tensor(q_f[k][:, :], bank[k][:, :], rinv[:, :], ALU.mult).then_inc(q_ready, 1)

            LOWEST = -3.0e38

            def top16(step, values, index, src, cut, n):
                for t in range(TC):
                    ins = dve.max(values[:, t, 0:8], src[:, t, 0:n])
                step(ins, max_next=True)
                for t in range(TC):
                    dve.max_index(index[:, t, 0:8], values[:, t, 0:8], src[:, t, 0:n])
                    ins = dve.match_replace(cut[:, t, 0:n], values[:, t, 0:8], src[:, t, 0:n], LOWEST)
                step(ins, max_next=True)
                for t in range(TC):
                    ins = dve.max(values[:, t, 8:16], cut[:, t, 0:n])
                step(ins, max_next=True)
                for t in range(TC):
                    ins = dve.max_index(index[:, t, 8:16], values[:, t, 8:16], cut[:, t, 0:n])
                step(ins)

            def half_topk(step, n, p):
                before_max(s_ready, n + 1)
                top16(step, t_v[p], t_i[p], s_f[p], s_cut, NK)
                step(dve.tensor_copy(t_if[p][:, :, :], t_i[p][:, :, :]))

            def best_pairs(step):
                step(dve.tensor_tensor(cand[:, :, :, :],
                                       t_v[0][:, :, :].unsqueeze(3).to_broadcast([P, TC, TOPK, TOPK]),
                                       t_v[1][:, :, :].unsqueeze(2).to_broadcast([P, TC, TOPK, TOPK]), ALU.add),
                     max_next=True)
                top16(step, b_v, b_pos, cand[:, :, :, :].rearrange("p t a b -> p t (a b)"), cand_cut, TOPK * TOPK)

            def keys_and_gates(step, hd):
                dve.tensor_tensor(b_exp[:, :, :], b_v[:, :, :], b_v[:, :, 0:1].to_broadcast([P, TC, TOPK]),
                                  ALU.subtract).then_inc(gate_in, 1)
                flat = b_pos[:, :, :].rearrange("p t k -> p (t k)")
                dve.tensor_scalar(pos_hl[0][:, :], flat, 4, None, ALU.logical_shift_right)
                step(dve.tensor_scalar(pos_hl[1][:, :], flat, 15, None, ALU.bitwise_and))
                for p in range(2):
                    dve.tensor_tensor(pick[p][:, :, :], pos_hl[p][:, :].unsqueeze(2).to_broadcast([P, TC * TOPK, TOPK]),
                                      iota[:, None, 0:TOPK].to_broadcast([P, TC * TOPK, TOPK]), ALU.is_equal)\
                       .then_inc(pick_ready, 1)
                dve.wait_ge(gate_exp, hd + 1)
                step(dve.tensor_reduce(b_sum[:, :], b_exp[:, :, :], AX.X, ALU.add))
                step(dve.reciprocal(b_inv[:, :], b_sum[:, :]))

                def chosen(i):
                    if isinstance(hd, int):
                        return sel[i][:, :, hd, :]
                    return sel[i][:, :, bass.ds(hd, 1), :].rearrange("p t a k -> p t (a k)")

                step(dve.tensor_tensor(chosen(2), b_exp[:, :, :], b_inv[:, :].unsqueeze(2).to_broadcast([P, TC, TOPK]),
                                       ALU.mult))
                dve.wait_ge(picked_ready, 2 * hd + 2)
                for p in range(2):
                    ins = dve.tensor_reduce(chosen(p), picked[p][:, :, :].rearrange("p (t k) m -> p t k m", t=TC),
                                            AX.X, ALU.add)
                step(ins)

            lo(U_WQ + 1, (U_WQ + 1) % 2)
            inverse(3, rinv, D)
            query_out(0, 0, U_WQ)
            lo(U_WQ + 2, U_WQ % 2)
            query_out(1, 1, U_WQ + 1)
            with dve.Fori(1, PH) as i:
                u = 4 * i + U_WQ - 2
                step, k = step_by_step(PER_TOPK * (i - 1))
                lo(u + 1, (U_WQ + 1) % 2)
                half_topk(step, 2 * i - 2, 0)
                query_out(2 * i, 0, u)
                lo(u + 2, U_WQ % 2)
                half_topk(step, 2 * i - 1, 1)
                lo(u + 3, (U_WQ + 1) % 2)
                best_pairs(step)
                query_out(2 * i + 1, 1, u + 2)
                lo(u + 4, U_WQ % 2)
                keys_and_gates(step, i - 1)
                assert k[0] == PER_TOPK
            step, k = step_by_step(PER_TOPK * (PH - 1))
            half_topk(step, 2 * PH - 2, 0)
            half_topk(step, 2 * PH - 1, 1)
            best_pairs(step)
            keys_and_gates(step, PH - 1)

            def one_hots(q, s, first=False):
                o = [P, OH, NK]
                if first and q == 0:
                    dve.wait_ge(lo_ready, 2 * U_BLOCK + 2)
                if not first:
                    dve.wait_ge(oh_g, q - 1)
                dve.tensor_tensor(one_i[s][:, :, :], iota[:, None, :].to_broadcast(o),
                                  hk_t[0][:, bass.ds(OH * q, OH)].unsqueeze(2).to_broadcast(o), ALU.is_equal)\
                   .then_inc(oh_i, 1)
                if not first:
                    dve.wait_ge(g_done, 2 * q - 2)
                dve.tensor_tensor(one_j[s][:, :, :], iota[:, None, :].to_broadcast(o),
                                  hk_t[1][:, bass.ds(OH * q, OH)].unsqueeze(2).to_broadcast(o), ALU.is_equal)\
                   .then_inc(oh_j, 1)

            dve.wait_ge(hk_ready, 3)

            def g_block(b, s, first=False):
                for e in range(TB // OH):
                    one_hots((TB // OH) * b + e, e % 2, first=first and e < 2)
                    if e in (1, 2):
                        lo(b + U_BLOCK + 1, (U_BLOCK + 1 + s) % 2, halves=(e - 1,))

            g_block(0, 0, first=True)
            g_block(1, 1)
            with dve.Fori(1, N_TB // 2) as b2:
                for s in range(2):
                    g_block(2 * b2 + s, s)

            def scale(j, m, par, n, u=None, b=None):
                if m == GROUP - 1:
                    dve.wait_ge(h_in[par], 16 * n + 16)
                    scores = h_pre[par]
                else:
                    dve.wait_ge(weights_used, u + 1)
                    scores = bank[b]
                dve.tensor_tensor(h_s[:, :], scores[:, :], rinv[:, :], ALU.mult).then_inc(e_scaled, 1)

            def gate(j, m, par, n):
                dve.wait_ge(e_gelu, j + 1)
                dve.wait_ge(g_in[par], 16 * n + 16)
                dve.tensor_tensor(h_a[:, :].rearrange("p (b t) -> p b t", t=TB),
                                  h_g[:, :].rearrange("p (b t) -> p b t", t=TB), g_tile[par][:, :, m, :], ALU.mult)\
                   .then_inc(e_gated, 1)
                a = a_slot(m, par)
                dve.wait_ge(e_hi, j + 1)
                dve.tensor_tensor(a_lo[a][:, :], h_a[:, :], a_hi[a][:, :].bitcast(F32), ALU.subtract)\
                   .then_inc(e_ready, 1)

            def activated(j, m, par, n, u=None, b=None):
                scale(j, m, par, n, u, b)
                gate(j, m, par, n)

            def peer_group(g, g2, par, first=False, last=False):
                p = g * GROUP + 1
                if first:
                    lo(peer_unit(g, 1), peer_slot(1, par))
                    scale(0, 0, par, g2, U_PEER, 0)
                    lo(peer_unit(g, 2), peer_slot(2, par))
                    dve.wait_ge(e_gelu, 1)
                    scale(p, 1, par, g2, peer_unit(g, 0), 1)
                    gate(0, 0, par, g2)
                    dve.wait_ge(e_ready, 1)
                    gate(p, 1, par, g2)
                else:
                    lo(peer_unit(g, 1), peer_slot(1, par))
                    activated(p, 1, par, g2, peer_unit(g, 0), (1 + par) % 2)
                    lo(peer_unit(g, 2), peer_slot(2, par))
                activated(p + 1, 3, par, g2)
                activated(p + 2, 2, par, g2, peer_unit(g, 1), (2 + par) % 2)
                if not last:
                    lo(peer_unit(g, 3), peer_slot(3, par))
                    activated(p + 3, 0, 1 - par, g2 + par, peer_unit(g, 2), (3 + par) % 2)
                for q in range(4):
                    k = 3 + q - (1 if last else 0)
                    lo(peer_unit(g, k + 1), peer_slot(k + 1, par), halves=(0,))
                    for c in range(4):
                        if c < 3:
                            dve.wait_ge(v_done, 12 * g + 3 * q + c + 1)
                        else:
                            dve.wait_ge(weights_used, peer_unit(g, k) + 1)
                        hc = h[:, 4 * q + c, :]
                        dve.tensor_tensor(hc, bank[2 + c][:, :], hc, ALU.add).then_inc(v_added, 1)
                        if c == 0:
                            lo(peer_unit(g, k + 1), peer_slot(k + 1, par), halves=(1,))
                    if last:
                        for c in range(4 * q, 4 * q + 4):
                            third_lo(c)

            def third_lo(c):
                dve.wait_ge(x3_hi_ready, c + 1)
                dve.scalar_tensor_tensor(x2_lo[:, c, :], h[:, c, :],
                                         gain[:, G_PLE - C_GAIN + c:G_PLE - C_GAIN + c + 1],
                                         x2_hi[:, c, :].bitcast(F32), ALU.mult, ALU.subtract).then_inc(x3_ready, 1)

            for s in range(2):
                dve.wait_ge(g_stored[s], 16 * (N_TB // 2))
            acc_clear()
            peer_group(0, 0, 0, first=True)
            for c in range(2):
                dve.wait_ge(p_hi, c + 1)
                dve.tensor_tensor(pt_lo[:, c, :], pt[:, c, :], pt_hi[:, c, :].bitcast(F32), ALU.subtract)\
                   .then_inc(p_ready, 1)
            peer_group(1, 0, 1)
            with dve.Fori(1, N_GROUPS // 2 - 1) as g2:
                peer_group(2 * g2, g2, 0)
                peer_group(2 * g2 + 1, g2, 1)
            peer_group(N_GROUPS - 2, N_GROUPS // 2 - 1, 0)
            peer_group(N_GROUPS - 1, N_GROUPS // 2 - 1, 1, last=True)

            lo(U_PROJ + 1, (U_PROJ + 1) % 2)
            for n in range(1, DC, 2):
                if n == 9:
                    lo(U_GATE, U_GATE % 2)
                if n % 8 == 7:
                    dve.wait_ge(weights_used, U_PROJ + n // 8 + 1)
                else:
                    dve.wait_ge(proj_done, n + 1 - n // 8)
                dve.tensor_copy(proj[:, n, :], bank[n % 4][:, :]).then_inc(dve_proj_out, 1)
            lo(U_GATE + 1, (U_GATE + 1) % 2)
            inverse(4, rinv, D)
            acc_clear()

            def gate_out(n, k, more=True):
                if more:
                    lo(n + U_GATE + 1, (U_GATE + 1 + k) % 2)
                dve.wait_ge(weights_used, n + U_GATE + 1)
                dve.tensor_tensor(g_pre[:, :], bank[k][:, :], rinv[:, :], ALU.mult).then_inc(gate_pre, 1)
                dve.wait_ge(gate_sig, n + 1)
                dve.tensor_tensor(g_mul[:, :], g_sig[:, :], chunk(proj, n), ALU.mult).then_inc(gate_mul, 1)
                dve.wait_ge(gate_mul, n + 1)
                dve.tensor_tensor(chunk(h, n), chunk(h, n), g_mul[:, :], ALU.add).then_inc(h_end, 1)
                acc_add(2, n, 2 + k, end_sq)

            gate_out(0, 0, more=False)
            with dve.Fori(0, (DC - 2) // 2) as i:
                gate_out(2 * i + 1, 1)
                gate_out(2 * i + 2, 0)
            gate_out(DC - 1, 1, more=False)
            inverse(5, rinv, D)
            for c in range(DC):
                dve.scalar_tensor_tensor(proj[:, c, :], h[:, c, :],
                                         gain[:, G_FIN - C_GAIN + c:G_FIN - C_GAIN + c + 1], rinv[:, :],
                                         ALU.mult, ALU.mult).then_inc(fin_ready, 1)

        @block.gpsimd
        def _(pool):
            for c in range(1, DC):
                pool.wait_ge(sq_ready, c + 1)
                if c > 1:
                    pool.wait_ge(pool_step, c - 1)
                pool.tensor_tensor(x_acc[:, :], sq_x[:, 0, :] if c == 1 else x_acc[:, :], sq_x[:, c, :], ALU.add)\
                    .then_inc(pool_step, 1)

            steps = [0]

            def win_do(ins):
                steps[0] += 1
                ins.then_inc(win_step, 1)
                pool.wait_ge(win_step, steps[0])

            for g, w in enumerate(WINDOWS):
                if g:
                    pool.wait_ge(pooled, g)
                pool.wait_ge(in_out, 10 + g)
                src, i = z[:, 9 + g, :], 0
                for e in range(g + 1):
                    s = 2 ** e
                    win_do(pool.tensor_tensor(win[i][:, s:T], src[:, s:T], src[:, 0:T - s], ALU.add))
                    win_do(pool.tensor_copy(win[i][:, 0:s], src[:, 0:s]))
                    src, i = win[i][:, :], 1 - i
                win_do(pool.tensor_scalar(win[i][:, w:T], src[:, w:T], 1.0 / w, None, ALU.mult))
                win_do(pool.tensor_tensor(win[i][:, 0:w], src[:, 0:w], p_inv[:, g, 0:w], ALU.mult))
                pool.tensor_tensor(z[:, 9 + g, :], win[i][:, :], z[:, 9 + g, :], ALU.subtract).then_inc(pooled, 1)

            def copy_v(hd, k):
                pool.tensor_copy(v_h[k][:, :, :].rearrange("p c d -> p (c d)"), chunk(v_all, hd + 4))\
                    .then_inc(v_copied, 1)

            pool.wait_ge(v_out, 4 * N_V)
            copy_v(0, 0)
            copy_v(1, 1)
            with pool.Fori(1, HEADS // 2) as i:
                for k in range(2):
                    pool.wait_ge(mixed, 2 * i + k - 1)
                    copy_v(2 * i + k, k)

            def keys(hd):
                for p in range(2):
                    pool.wait_ge(pick_ready, 2 * hd + p + 1)
                    pool.tensor_tensor(
                        picked[p][:, :, :].rearrange("p (t k) m -> p t k m", t=TC),
                        pick[p][:, :, :].rearrange("p (t k) m -> p t k m", t=TC),
                        t_if[p][:, :, :].unsqueeze(2).to_broadcast([P, TC, TOPK, TOPK]), ALU.mult)\
                        .then_inc(picked_ready, 1)

            with pool.Fori(0, PH - 1) as hd:
                keys(hd)
            for u in range(U_ALONE + 1, U_ALONE + ALONE + 1):
                for s in range(2):
                    pool.wait_ge(hi_ready, 2 * u + s + 1)
                    pool.wait_ge(lo_ready, 2 * u + s)
                    pool.tensor_tensor(w_lo[u % 2][:, 8 * s:8 * s + 8, :], raw[s][:, :, :],
                                       w_hi[u % 2][:, 8 * s:8 * s + 8, :].bitcast(F32), ALU.subtract)\
                        .then_inc(lo_ready, 1)
            keys(PH - 1)

            def gated(q, s, first=False):
                pool.wait_ge(oh_i, q + 1)
                if not first:
                    pool.wait_ge(g_done, 2 * q - 2)
                pool.tensor_tensor(one_g[s][:, :, :], one_i[s][:, :, :],
                                   hk_t[2][:, bass.ds(OH * q, OH)].unsqueeze(2).to_broadcast([P, OH, NK]), ALU.mult)\
                    .then_inc(oh_g, 1)

            gated(0, 0, first=True)
            gated(1, 1, first=True)
            with pool.Fori(1, T // OH // 2) as q2:
                for s in range(2):
                    gated(2 * q2 + s, s)

            for c in range(DC):
                pool.wait_ge(h3_sq, c + 1)
                pool.wait_ge(acc_step, ACC + c + 1)
                pool.tensor_tensor(acc[:, :], acc[:, :], sq_h[c % 2][:, :], ALU.add).then_inc(acc_step, 1)


def _units(w, rows, cols):
    return np.ascontiguousarray(w.reshape(rows, P, cols, P).transpose(2, 1, 0, 3))


def _columns(g):
    return np.asarray(g).reshape(-1, P).T


def _constants():
    c = np.zeros((P, 4 * P), np.float32)
    r = np.arange(P)
    c[:, C_IDENT:C_IDENT + P] = np.eye(P)
    c[:, C_IOTA:C_IOTA + P] = r
    c[:, C_MASK:C_MASK + P] = np.where(r[None, :] <= r[:, None], 0.0, -1e30)
    c[:, C_DUP:C_DUP + P] = (r[:, None] % 64 == r[None, :] % 64)
    return c


def _rope_columns():
    freq = np.float32(10000.0) ** (-np.arange(0, 64, 2, dtype=np.float32) / np.float32(64))
    phase = np.repeat(np.array([np.pi / 2, np.pi / 2, np.pi, 0.0]), 32)
    return np.stack([np.tile(freq, 4), phase], 1).astype(np.float32)


def _pool_inverse():
    t = np.arange(16)
    return np.broadcast_to(np.stack([1.0 / np.minimum(t + 1, w) for w in WINDOWS])[None], (P, 4, 16)).astype(np.float32)


def kernel(x, p, positions, mix_norm_g, w_in, pool_w, pool_scale, q_norm_g, w_uq, kv_norm_g, w_ukv, w_o,
           ffn_norm_g, peer_wq, peer_sub_keys, peer_u, peer_v, ple_norm_g, ple_w_gate, ple_w_proj, final_norm_g):
    import concourse.bacc as bacc
    from concourse.bass_utils import run_bass_kernel_spmd

    a = np.asarray
    turn = np.r_[0:32, 32:64, 32:64, 0:32]
    w = a(w_in)[0]
    w = np.concatenate([w[:, 512:1536], w[:, 1536:1600][:, turn], w[:, 0:512]], 1)
    uq = a(w_uq)[0].reshape(LC, P, HEADS, QK)
    ukv = a(w_ukv)[0].reshape(LC, P, HEADS, 2 * P)
    head = np.concatenate([uq[..., :P], uq[..., P:][..., turn], ukv[..., :P]], 0)
    arrays = {
        "x_t": a(x)[0].T.reshape(DC, P, T).transpose(1, 0, 2),
        "p_t": a(p)[0, 0].T.reshape(2, P, T).transpose(1, 0, 2),
        "positions": a(positions),
        "gains": np.concatenate([_columns(g) for g in (mix_norm_g, ffn_norm_g, ple_norm_g, final_norm_g, q_norm_g,
                                                       kv_norm_g, pool_scale)], 1),
        "consts": _constants(),
        "rope_cols": _rope_columns(),
        "pool_inv": _pool_inverse(),
        "w_in": _units(w, DC, N_IN),
        "pool_w": a(pool_w)[0].transpose(1, 0, 2),
        "w_head": head.transpose(2, 1, 0, 3),
        "w_v": ukv[..., P:].reshape(LC, P, N_V, 4, P).transpose(2, 1, 0, 3, 4).reshape(N_V, P, 16, P),
        "w_o": _units(a(w_o)[0], DC, DC),
        "w_q": _units(a(peer_wq)[0], DC, DC),
        "keys": a(peer_sub_keys)[0].reshape(2 * PH, NK, P).transpose(2, 0, 1),
        "u_t": a(peer_u)[0].reshape(NK, NK, DC, P).transpose(0, 3, 2, 1),
        "v": a(peer_v)[0],
        "w_proj": a(ple_w_proj)[0].reshape(2, P, 2, 8, P).transpose(2, 1, 3, 0, 4).reshape(2, P, 16, P),
        "w_gate": _units(a(ple_w_gate)[0], DC, DC),
    }
    arrays = {n: np.ascontiguousarray(v) for n, v in arrays.items()}
    nc = bacc.Bacc("TRN2", target_bir_lowering=False, num_devices=1)
    aps = {n: nc.dram_tensor(f"in_{n}", v.shape, mybir.dt.from_np(v.dtype), kind="ExternalInput").ap()
           for n, v in arrays.items()}
    out = nc.dram_tensor("out_t", (P, DC, T), F32, kind="ExternalOutput").ap()
    build_block(nc, **aps, out_t=out)
    got = run_bass_kernel_spmd(nc, [{f"in_{n}": v for n, v in arrays.items()}], core_ids=[0])
    return got.results[0]["out_t"].transpose(2, 1, 0).reshape(1, T, D)
```
